# Optimizing a Trainium2 kernel written in Bass

```python
import jax
import jax.numpy as jnp
from jax import lax
import numpy as np

D_MODEL = 1024
BATCH = 1
SEQ = 256
DEPTH = 2

MIX = D_MODEL // 2
MOBA_HEAD_DIM = 64
MOBA_HEADS = MIX // MOBA_HEAD_DIM
MOBA_BLOCK = 256
MOBA_TOPK = 3
Q_BLOCK = 128
ROPE_THETA = 500000.0
ROPE_DIMS = MOBA_HEAD_DIM // 4
GLA_HEADS = 4
GLA_DK = MIX // 2
GLA_DV = MIX
GLA_GATE_RANK = 16
GLA_TAU = 16.0
GLA_CHUNK = 64
MLSTM_HEADS = 4
MLSTM_DQK = MIX
MLSTM_DV = MIX
MLSTM_CONV = 4
MLSTM_CHUNK = 64
N_BRANCHES = 3
D_FF = ((8 * D_MODEL // 3 + 255) // 256) * 256
N_EXPERTS = 8
TOP_K = 2
MOE_BLOCK = 256
EPS = 1e-6

IN_LAYOUT = (
    ('moba_q', MIX), ('moba_k', MIX), ('moba_v', MIX),
    ('gla_q', GLA_DK), ('gla_k', GLA_DK), ('gla_v', GLA_DV),
    ('gla_a', GLA_GATE_RANK), ('gla_r', GLA_DV),
    ('mlstm_q', MLSTM_DQK), ('mlstm_k', MLSTM_DQK), ('mlstm_v', MLSTM_DV),
    ('mlstm_i', MLSTM_HEADS), ('mlstm_f', MLSTM_HEADS), ('mlstm_o', MLSTM_DV),
    ('merge_gate', N_BRANCHES * D_MODEL),
)
N_IN = sum(size for _, size in IN_LAYOUT)

kernel_name = 'hybrid_moba_gla_mlstm_moe_block'

def _col_offset(name):
    off = 0
    for n, size in IN_LAYOUT:
        if n == name:
            return off
        off += size
    raise KeyError(name)

def _split_in(z):
    out = {}
    off = 0
    for n, size in IN_LAYOUT:
        out[n] = z[..., off:off + size]
        off += size
    return out

def rmsnorm(x, g):
    xf = x.astype(jnp.float32)
    y = xf * lax.rsqrt(jnp.mean(xf * xf, axis=-1, keepdims=True) + EPS)
    return (y * g.astype(jnp.float32)).astype(x.dtype)

def to_heads(t, nh):
    b, s, _ = t.shape
    return t.reshape(b, s, nh, -1).transpose(0, 2, 1, 3)

def from_heads(t):
    b, nh, s, hd = t.shape
    return t.transpose(0, 2, 1, 3).reshape(b, s, nh * hd)

def partial_rope(x, pos):
    half = ROPE_DIMS // 2
    inv_freq = jnp.power(ROPE_THETA, -jnp.arange(half, dtype=jnp.float32) * 2.0 / ROPE_DIMS)
    ang = pos.astype(jnp.float32)[:, None] * inv_freq[None, :]
    cos, sin = jnp.cos(ang), jnp.sin(ang)
    xr = x[..., :ROPE_DIMS].astype(jnp.float32)
    x1, x2 = xr[..., :half], xr[..., half:]
    rot = jnp.concatenate([x1 * cos - x2 * sin, x2 * cos + x1 * sin], axis=-1)
    return jnp.concatenate([rot.astype(x.dtype), x[..., ROPE_DIMS:]], axis=-1)

def moba_attention(q, k, v):
    f32 = jnp.float32
    b, nh, s, hd = q.shape
    nb = -(-s // MOBA_BLOCK)
    n_sel = min(MOBA_TOPK, nb)
    pad = nb * MOBA_BLOCK - s
    kb = jnp.pad(k, ((0, 0), (0, 0), (0, pad), (0, 0))).reshape(b, nh, nb, MOBA_BLOCK, hd)
    vb = jnp.pad(v, ((0, 0), (0, 0), (0, pad), (0, 0))).reshape(b, nh, nb, MOBA_BLOCK, hd)
    k_mean = jnp.mean(kb.astype(f32), axis=3)
    nq = s // Q_BLOCK
    q_blocks = q.reshape(b, nh, nq, Q_BLOCK, hd).transpose(2, 0, 1, 3, 4)
    bi = jnp.arange(b)[:, None, None, None]
    hi = jnp.arange(nh)[None, :, None, None]
    blk_ids = jnp.arange(nb)
    scale = hd ** -0.5
    n_cols = n_sel * MOBA_BLOCK

    def one_block(args):
        qb, c = args
        q_pos = c * Q_BLOCK + jnp.arange(Q_BLOCK)
        cur = (c * Q_BLOCK) // MOBA_BLOCK
        gate = jnp.einsum('bhqd,bhnd->bhqn', qb.astype(f32), k_mean)
        gate = jnp.where(blk_ids < cur, gate, -jnp.inf)
        _, sel = lax.top_k(gate, n_sel)
        sel_ok = jnp.arange(n_sel) < cur
        k_sel = kb[bi, hi, sel]
        v_sel = vb[bi, hi, sel]
        s_sel = jnp.einsum('bhqd,bhqrtd->bhqrt', qb, k_sel).astype(f32) * scale
        s_sel = jnp.where(sel_ok[:, None], s_sel, -jnp.inf)
        k_own = lax.dynamic_index_in_dim(kb, cur, axis=2, keepdims=False)
        v_own = lax.dynamic_index_in_dim(vb, cur, axis=2, keepdims=False)
        s_own = jnp.einsum('bhqd,bhtd->bhqt', qb, k_own).astype(f32) * scale
        own_pos = cur * MOBA_BLOCK + jnp.arange(MOBA_BLOCK)
        s_own = jnp.where(own_pos[None, :] <= q_pos[:, None], s_own, -jnp.inf)
        p = jax.nn.softmax(jnp.concatenate([s_sel.reshape(b, nh, Q_BLOCK, n_cols), s_own], axis=-1), axis=-1)
        p_sel = p[..., :n_cols].reshape(b, nh, Q_BLOCK, n_sel, MOBA_BLOCK).astype(v.dtype)
        p_own = p[..., n_cols:].astype(v.dtype)
        return (jnp.einsum('bhqrt,bhqrtd->bhqd', p_sel, v_sel)
                + jnp.einsum('bhqt,bhtd->bhqd', p_own, v_own))

    out = lax.map(one_block, (q_blocks, jnp.arange(nq)))
    return out.transpose(1, 2, 0, 3, 4).reshape(b, nh, s, hd)

def gla_chunked(q, k, v, log_a):
    b, nh, s, dk = q.shape
    dv = v.shape[-1]
    L = GLA_CHUNK
    nc = s // L
    q = q * dk ** -0.5
    qc = q.reshape(b, nh, nc, L, dk)
    kc = k.reshape(b, nh, nc, L, dk)
    vc = v.reshape(b, nh, nc, L, dv)
    cum = jnp.cumsum(log_a.reshape(b, nh, nc, L, dk), axis=3)
    cum_last = cum[:, :, :, -1:, :]
    q_dec = qc * jnp.exp(cum)
    k_inv = kc * jnp.exp(-cum)
    k_to_end = kc * jnp.exp(cum_last - cum)
    causal = jnp.tril(jnp.ones((L, L), dtype=bool))
    att = jnp.where(causal, jnp.einsum('bhcid,bhcjd->bhcij', q_dec, k_inv), 0.0)
    o_intra = jnp.einsum('bhcij,bhcje->bhcie', att, vc)

    def step(state, inp):
        dec, kk, vv = inp
        new = dec[..., None] * state + jnp.einsum('bhjd,bhje->bhde', kk, vv)
        return new, state

    xs = (jnp.exp(cum_last[:, :, :, 0, :]).transpose(2, 0, 1, 3),
          k_to_end.transpose(2, 0, 1, 3, 4), vc.transpose(2, 0, 1, 3, 4))
    _, s_prev = lax.scan(step, jnp.zeros((b, nh, dk, dv), jnp.float32), xs)
    o_inter = jnp.einsum('bhcid,cbhde->bhcie', q_dec, s_prev)
    return (o_intra + o_inter).reshape(b, nh, s, dv)

def mlstm_chunked(q, k, v, i_pre, f_pre):
    b, nh, s, dk = q.shape
    dv = v.shape[-1]
    L = MLSTM_CHUNK
    nc = s // L
    k = k * dk ** -0.5
    qc = q.reshape(b, nh, nc, L, dk)
    kc = k.reshape(b, nh, nc, L, dk)
    vc = v.reshape(b, nh, nc, L, dv)
    ic = i_pre.reshape(b, nh, nc, L)
    cum = jnp.cumsum(jax.nn.log_sigmoid(f_pre).reshape(b, nh, nc, L), axis=-1)
    cum_last = cum[..., -1]
    a_end = cum_last[..., None] - cum + ic

    def step(carry, inp):
        c_st, n_st, m_st = carry
        bl, aa, kk, vv = inp
        m_new = jnp.maximum(bl + m_st, jnp.max(aa, axis=-1))
        w = jnp.exp(aa - m_new[..., None])
        dec = jnp.exp(bl + m_st - m_new)
        c_new = dec[..., None, None] * c_st + jnp.einsum('bhj,bhjd,bhje->bhde', w, kk, vv)
        n_new = dec[..., None] * n_st + jnp.einsum('bhj,bhjd->bhd', w, kk)
        return (c_new, n_new, m_new), (c_st, n_st, m_st)

    init = (jnp.zeros((b, nh, dk, dv), jnp.float32), jnp.zeros((b, nh, dk), jnp.float32),
            jnp.zeros((b, nh), jnp.float32))
    xs = (cum_last.transpose(2, 0, 1), a_end.transpose(2, 0, 1, 3),
          kc.transpose(2, 0, 1, 3, 4), vc.transpose(2, 0, 1, 3, 4))
    _, (c_prev, n_prev, m_prev) = lax.scan(step, init, xs)
    c_prev = c_prev.transpose(1, 2, 0, 3, 4)
    n_prev = n_prev.transpose(1, 2, 0, 3)
    m_prev = m_prev.transpose(1, 2, 0)
    causal = jnp.tril(jnp.ones((L, L), dtype=bool))
    log_d = jnp.where(causal, cum[..., :, None] - cum[..., None, :] + ic[..., None, :], -jnp.inf)
    log_inter = cum + m_prev[..., None]
    m_i = jnp.maximum(log_inter, jnp.max(log_d, axis=-1))
    w_intra = jnp.einsum('bhcid,bhcjd->bhcij', qc, kc) * jnp.exp(log_d - m_i[..., None])
    w_inter = jnp.exp(log_inter - m_i)
    num = (w_inter[..., None] * jnp.einsum('bhcid,bhcde->bhcie', qc, c_prev)
           + jnp.einsum('bhcij,bhcje->bhcie', w_intra, vc))
    den = w_inter * jnp.einsum('bhcid,bhcd->bhci', qc, n_prev) + jnp.sum(w_intra, axis=-1)
    h = num / jnp.maximum(jnp.abs(den), jnp.exp(-m_i))[..., None]
    return h.reshape(b, nh, s, dv)

def causal_depthwise_conv(x, w, bias):
    y = lax.conv_general_dilated(x, w[:, None, :], window_strides=(1,),
                                 padding=[(w.shape[0] - 1, 0)],
                                 dimension_numbers=('NWC', 'WIO', 'NWC'),
                                 feature_group_count=x.shape[-1])
    return y + bias

def hybrid_mixer(h, w_in, b_in, mlstm_conv_w, mlstm_conv_b, gla_gate_w, gla_gate_b,
                 gla_norm_g, w_up_moba, w_up_gla, w_up_mlstm, w_o):
    f32 = jnp.float32
    dt = h.dtype
    b, s, _ = h.shape
    z = _split_in(h @ w_in + b_in)
    pos = jnp.arange(s)

    q = partial_rope(to_heads(z['moba_q'], MOBA_HEADS), pos)
    k = partial_rope(to_heads(z['moba_k'], MOBA_HEADS), pos)
    y_moba = from_heads(moba_attention(q, k, to_heads(z['moba_v'], MOBA_HEADS)))

    log_a = jax.nn.log_sigmoid((z['gla_a'] @ gla_gate_w + gla_gate_b).astype(f32)) / GLA_TAU
    o = gla_chunked(to_heads(z['gla_q'], GLA_HEADS).astype(f32), to_heads(z['gla_k'], GLA_HEADS).astype(f32),
                    to_heads(z['gla_v'], GLA_HEADS).astype(f32), to_heads(log_a, GLA_HEADS))
    o = o * lax.rsqrt(jnp.mean(o * o, axis=-1, keepdims=True) + EPS)
    y_gla = (from_heads(o) * gla_norm_g.astype(f32) * jax.nn.silu(z['gla_r'].astype(f32))).astype(dt)

    qk = jax.nn.silu(causal_depthwise_conv(jnp.concatenate([z['mlstm_q'], z['mlstm_k']], axis=-1),
                                           mlstm_conv_w, mlstm_conv_b))
    mq, mk = qk[..., :MLSTM_DQK], qk[..., MLSTM_DQK:]
    hm = mlstm_chunked(to_heads(mq, MLSTM_HEADS).astype(f32), to_heads(mk, MLSTM_HEADS).astype(f32),
                       to_heads(z['mlstm_v'], MLSTM_HEADS).astype(f32),
                       z['mlstm_i'].astype(f32).transpose(0, 2, 1), z['mlstm_f'].astype(f32).transpose(0, 2, 1))
    y_mlstm = (from_heads(hm) * jax.nn.sigmoid(z['mlstm_o'].astype(f32))).astype(dt)

    g = jax.nn.sigmoid(z['merge_gate'].astype(f32)).astype(dt).reshape(b, s, N_BRANCHES, D_MODEL)
    merged = (g[:, :, 0] * (y_moba @ w_up_moba) + g[:, :, 1] * (y_gla @ w_up_gla)
              + g[:, :, 2] * (y_mlstm @ w_up_mlstm))
    return merged @ w_o

def swiglu(x, w_gate, w_up, w_down):
    return (jax.nn.silu(x @ w_gate) * (x @ w_up)) @ w_down

def moe_swiglu(x, router_w, router_b, w_gate, w_up, w_down):
    b, s, d = x.shape
    t = b * s
    xt = x.reshape(t, d)
    logits = (xt @ router_w).astype(jnp.float32) + router_b.astype(jnp.float32)
    top_logit, top_e = lax.top_k(logits, TOP_K)
    gate = jax.nn.softmax(top_logit, axis=-1)
    n_pairs = t * TOP_K
    e_flat = top_e.reshape(n_pairs)
    tok_flat = jnp.repeat(jnp.arange(t, dtype=jnp.int32), TOP_K)
    g_flat = gate.reshape(n_pairs)
    order = jnp.argsort(e_flat)
    e_s, tok_s, g_s = e_flat[order], tok_flat[order], g_flat[order]
    counts = jnp.bincount(e_flat, length=N_EXPERTS)
    starts = jnp.cumsum(counts) - counts
    padded = (counts + MOE_BLOCK - 1) // MOE_BLOCK * MOE_BLOCK
    pad_ends = jnp.cumsum(padded)
    pad_starts = pad_ends - padded
    dest = pad_starts[e_s] + jnp.arange(n_pairs) - starts[e_s]
    n_rows = ((n_pairs + MOE_BLOCK - 1) // MOE_BLOCK + N_EXPERTS) * MOE_BLOCK
    n_blk = n_rows // MOE_BLOCK
    rows_tok = jnp.full((n_rows,), t, jnp.int32).at[dest].set(tok_s)
    rows_g = jnp.zeros((n_rows,), x.dtype).at[dest].set(g_s.astype(x.dtype))
    blk_e = jnp.minimum(jnp.searchsorted(pad_ends, jnp.arange(n_blk) * MOE_BLOCK, side='right'),
                        N_EXPERTS - 1)
    x_pad = jnp.concatenate([xt, jnp.zeros((1, d), xt.dtype)], axis=0)

    def block(args):
        tok, e = args
        xb = x_pad[tok]
        return swiglu(xb, w_gate[e], w_up[e], w_down[e])

    y_rows = lax.map(block, (rows_tok.reshape(n_blk, MOE_BLOCK), blk_e)).reshape(n_rows, d)
    y_rows = y_rows * rows_g[:, None]
    out = jnp.zeros((t + 1, d), x.dtype).at[rows_tok].add(y_rows)[:t]
    return out.reshape(b, s, d)

def setup_inputs(seed: int = 0) -> dict:
    key = jax.random.key(seed)
    ks = jax.random.split(key, 26)
    f32 = jnp.float32

    def nrm(k, shape, scale):
        return jax.random.normal(k, shape, f32) * scale

    n_dense = (DEPTH + 1) // 2
    n_moe = DEPTH // 2
    f_off = _col_offset('mlstm_f')
    b_in = nrm(ks[3], (DEPTH, N_IN), 0.02)
    b_in = b_in.at[:, f_off:f_off + MLSTM_HEADS].add(jnp.linspace(3.0, 6.0, MLSTM_HEADS))
    return {
        'x': nrm(ks[0], (BATCH, SEQ, D_MODEL), 1.0),
        'attn_norm_g': 1.0 + nrm(ks[1], (DEPTH, D_MODEL), 0.02),
        'w_in': nrm(ks[2], (DEPTH, D_MODEL, N_IN), D_MODEL ** -0.5),
        'b_in': b_in,
        'mlstm_conv_w': nrm(ks[4], (DEPTH, MLSTM_CONV, 2 * MLSTM_DQK), MLSTM_CONV ** -0.5),
        'mlstm_conv_b': nrm(ks[5], (DEPTH, 2 * MLSTM_DQK), 0.02),
        'gla_gate_w': nrm(ks[6], (DEPTH, GLA_GATE_RANK, GLA_DK), GLA_GATE_RANK ** -0.5),
        'gla_gate_b': nrm(ks[7], (DEPTH, GLA_DK), 0.02),
        'gla_norm_g': 1.0 + nrm(ks[8], (DEPTH, GLA_DV), 0.02),
        'w_up_moba': nrm(ks[9], (DEPTH, MIX, D_MODEL), MIX ** -0.5),
        'w_up_gla': nrm(ks[10], (DEPTH, MIX, D_MODEL), MIX ** -0.5),
        'w_up_mlstm': nrm(ks[11], (DEPTH, MIX, D_MODEL), MIX ** -0.5),
        'w_o': nrm(ks[12], (DEPTH, D_MODEL, D_MODEL), D_MODEL ** -0.5),
        'ffn_norm_g': 1.0 + nrm(ks[13], (DEPTH, D_MODEL), 0.02),
        'ffn_w_gate': nrm(ks[14], (n_dense, D_MODEL, D_FF), D_MODEL ** -0.5),
        'ffn_w_up': nrm(ks[15], (n_dense, D_MODEL, D_FF), D_MODEL ** -0.5),
        'ffn_w_down': nrm(ks[16], (n_dense, D_FF, D_MODEL), D_FF ** -0.5),
        'router_w': nrm(ks[17], (n_moe, D_MODEL, N_EXPERTS), D_MODEL ** -0.5),
        'router_b': nrm(ks[18], (n_moe, N_EXPERTS), 0.01),
        'moe_w_gate': nrm(ks[19], (n_moe, N_EXPERTS, D_MODEL, D_FF), D_MODEL ** -0.5),
        'moe_w_up': nrm(ks[20], (n_moe, N_EXPERTS, D_MODEL, D_FF), D_MODEL ** -0.5),
        'moe_w_down': nrm(ks[21], (n_moe, N_EXPERTS, D_FF, D_MODEL), D_FF ** -0.5),
        'final_norm_g': 1.0 + nrm(ks[22], (D_MODEL,), 0.02),
    }

def reference(x, attn_norm_g, w_in, b_in, mlstm_conv_w, mlstm_conv_b, gla_gate_w, gla_gate_b,
              gla_norm_g, w_up_moba, w_up_gla, w_up_mlstm, w_o, ffn_norm_g, ffn_w_gate, ffn_w_up,
              ffn_w_down, router_w, router_b, moe_w_gate, moe_w_up, moe_w_down, final_norm_g):
    for l in range(DEPTH):
        h = rmsnorm(x, attn_norm_g[l])
        x = x + hybrid_mixer(h, w_in[l], b_in[l], mlstm_conv_w[l], mlstm_conv_b[l], gla_gate_w[l],
                             gla_gate_b[l], gla_norm_g[l], w_up_moba[l], w_up_gla[l], w_up_mlstm[l], w_o[l])
        h = rmsnorm(x, ffn_norm_g[l])
        j = l // 2
        if l % 2 == 0:
            x = x + swiglu(h, ffn_w_gate[j], ffn_w_up[j], ffn_w_down[j])
        else:
            x = x + moe_swiglu(h, router_w[j], router_b[j], moe_w_gate[j], moe_w_up[j], moe_w_down[j])
    return rmsnorm(x, final_norm_g)


_drawn_inputs = setup_inputs


def setup_inputs(seed=0):
    import zlib

    import numpy as np

    out = dict(_drawn_inputs(seed))
    spreads = {}
    factors = {'mlstm_conv_b': 8.0, 'gla_gate_b': 4.468, 'final_norm_g': 2.832}
    for name, (base, spread) in spreads.items():
        noise = np.random.default_rng([zlib.crc32(name.encode()), seed]).standard_normal(out[name].shape)
        drawn = base * np.exp(spread * noise) if base else spread * noise
        out[name] = jnp.asarray(drawn.astype(out[name].dtype))
    for name, factor in factors.items():
        out[name] = (out[name] * factor).astype(out[name].dtype)
    return out
```

```python
import numpy as np


def program(nc, x, w_in, b_in, cols_d, w_small_d, b_small_d, gate_w, w_up, w_o, ffn_gate, ffn_up, ffn_down,
            router_d, router_b, moe_gate, moe_up, moe_down, ffn_norm_g, final_g, rope_d, out):
    import concourse.bass as bass
    from concourse import mybir
    from contextlib import ExitStack

    f32, f32r, bf16 = mybir.dt.float32, mybir.dt.float32r, mybir.dt.bfloat16
    i8, i32, u32 = mybir.dt.int8, mybir.dt.int32, mybir.dt.uint32
    ACT, ALU, AX = mybir.ActivationFunctionType, mybir.AluOpType, mybir.AxisListType.X

    P = 128
    T, D = x.shape
    NT = T // P
    L = w_in.shape[0]
    MIX = D // 2
    KT = D // P
    F = ffn_gate.shape[1]
    E = moe_gate.shape[0]
    HD = 64
    GD = 64
    CH = 64
    MD = 128
    NHM = 4
    EPS = 1e-6
    TAU = 16.0
    W = 512
    CK = 2048
    names = (("mq", MIX), ("mk", MIX), ("mv", MIX), ("gqk", MIX), ("gv", MIX), ("ga", 16), ("gr", MIX),
             ("lq", MIX), ("lk", MIX), ("lv", MIX), ("li", 4), ("lf", 4), ("lo", MIX), ("mg", 3 * D))
    OFF, at_col = {}, 0
    for name, size in names:
        OFF[name] = at_col
        at_col += size
    C_AG, C_FG, C_CW, C_CB, C_BG, C_BL, C_GB, C_GN = 0, 8, 16, 48, 56, 60, 68, 70
    NCOL = cols_d.shape[2]

    UNITS = [("mq", OFF["mq"]), ("mk", OFF["mk"]), ("mv", OFF["mv"]), ("gqk", OFF["gqk"]), ("gv", OFF["gv"]),
             ("gr", OFF["gr"]), ("lq", OFF["lq"]), ("lk", OFF["lk"]), ("lv", OFF["lv"]), ("lo", OFF["lo"])]
    for b in range(3):
        UNITS += [(f"g{b}", OFF["mg"] + b * D), (f"g{b}'", OFF["mg"] + b * D + W), (f"up{b}", b)]
    UNITS += [("wo", 0), ("wo'", W)]
    UIDX = {name: i for i, (name, _) in enumerate(UNITS)}
    FEATURE_MAJOR = ("gqk", "lq", "lk")
    BIASED = [n for n, _ in UNITS if n[:2] not in ("up", "wo") and n not in FEATURE_MAJOR]
    NU = len(UNITS)
    NF = F // 256
    FFC = 3 * NF
    LAYER_BASE = [0, 2 * NU + FFC]
    MOE_BASE = LAYER_BASE[1] + 2 * NU
    RM, RE, RS = 3, 11, 3
    assert FFC % RE == 0 and FFC % RS == 0 and MOE_BASE % RS == 0 and L == 2 and F % 256 == 0

    FF = []
    for i in range(NF + 1):
        if i < NF:
            FF += [("gu", i, 0), ("gu", i, 1)]
        if i:
            FF += [("dn", i - 1, 0)]

    FILL, nfill = {}, [0] * 8

    def fills(l, tag, banks):
        for i, b in enumerate(banks):
            FILL[l, tag, i] = (b, nfill[b])
            nfill[b] += 1

    A4 = (4, 5, 6, 7)
    for l in range(L):
        for tag, banks in (
                ("norm", A4), ("mq", (0, 1)), ("mk", (2, 3)), ("small", (4,)), ("mv", (0, 1)), ("smallT", (5, 6)),
                ("qkT", A4), ("gqk", (2, 3)), ("gv", (0, 1)), ("s0", A4), ("gr", (2, 3)), ("s1", A4),
                ("lq", (0, 1)), ("pT0", A4), ("pv0", (4, 5)), ("lk", (2, 3)), ("pT1", A4), ("pv1", (4, 5)),
                ("ga", (7,)), ("lv", (0, 1)), ("yT0", (4, 5)), ("lo", (2, 3)), ("gs", A4), ("g0", (0, 1)),
                ("go", (4, 5)), ("g0'", (2, 3)), ("mb", (4, 5, 6)), ("up0", (0, 1, 2, 3)), ("yT1", (4, 5)),
                ("ms", A4), ("g1", (0, 1)), ("g1'", (2, 3)), ("mo", (4, 5, 6)), ("up1", (0, 1, 2, 3)),
                ("yT2", (4, 5)), ("g2", (0, 1)), ("g2'", (2, 3)), ("up2", (0, 1, 2, 3)), ("mgT", A4),
                ("wo", (0, 1)), ("wo'", (2, 3)), ("fnorm", A4)):
            fills(l, tag, banks)
        if l == 0:
            for i in range(NF):
                fills(0, f"gu{i}", (0, 1))
                fills(0, f"hT{i}", (2,))
            fills(0, "acc", A4)
    fills(1, "logits", (0,))
    fills(1, "rank", (1,))
    EXPERT, nexp = {}, [0] * 8

    def efills(tag, banks):
        for i, b in enumerate(banks):
            EXPERT[tag, i] = (b, nexp[b])
            nexp[b] += 1

    for i in range(NF):
        efills(f"gu{i}", (i % 2,))
        efills(f"hT{i}", (2,))
    efills("selT", (3,))
    efills("acc", (4, 5))
    efills("sc0", (6, 7))
    efills("sc1", (6, 7))
    efills("gather", (6, 7))
    PRO, EPI = {6: 1, 7: 1}, {6: 2, 7: 2}
    PASS_FILL = [[nfill[b] for b in range(8)]]
    PASS_FILL.append([PASS_FILL[0][b] + E * nexp[b] + PRO.get(b, 0) + EPI.get(b, 0) for b in range(8)])

    USED, n_used = [], 0
    for l in range(L):
        for name, _ in UNITS:
            n_used += 1
            USED.append(("w", n_used))
            USED.append(("bank", (l, name, 3 if name[:2] == "up" else 1)))
        if l == 0:
            for kind, i, c in FF:
                if kind == "gu" and c == 1:
                    USED.append(("bank", (0, f"gu{i}", 1)))
                elif kind == "dn" and i == NF - 1:
                    USED.append(("bank", (0, "acc", 3)))
                else:
                    n_used += 1
                    USED.append(("w", n_used))
    MOE_USED0 = n_used
    EUSED, eu = [], 0
    for kind, i, c in FF:
        if kind == "gu" and c == 1:
            EUSED.append(("bank", (f"gu{i}", 0)))
        elif kind == "dn" and i == NF - 1:
            EUSED.append(("bank", ("acc", 1)))
        else:
            eu += 1
            EUSED.append(("w", eu))
    EU = eu

    ctx = ExitStack()
    with ctx:
        def sb(name, shape, dt=f32):
            return ctx.enter_context(nc.sbuf_tensor(name, shape, dt))

        def sem(name):
            return ctx.enter_context(nc.semaphore(name))

        raw_m = sb("raw_m", [P, RM, CK])
        late = sb("late", [P, (RE - RM) * CK])
        w_hi = sb("w_hi", [P, RS, CK], f32r)
        w_lo = sb("w_lo", [P, RS, CK], f32r)
        xt = sb("xt", [P, NT, D])
        xn = sb("xn", [P, NT, D])
        hT_hi = sb("hT_hi", [P, KT, T], f32r)
        hT_lo = sb("hT_lo", [P, KT, T], f32r)
        yT_hi = sb("yT_hi", [P, 4, T], f32r)
        yT_lo = sb("yT_lo", [P, 4, T], f32r)
        ytok = sb("ytok", [P, NT, MIX])
        bias = sb("bias", [P, 3, W])
        tmp = sb("tmp", [P, 3072])
        ident = sb("ident", [P, P])
        cols = sb("cols", [P, L, NCOL])
        bsm = sb("bsm", [P, L, 24])
        ones_row = sb("ones_row", [4, T], bf16)
        ws_hi = sb("ws_hi", [P, KT * 24], f32r)
        ws_lo = sb("ws_lo", [P, KT * 24], f32r)
        cmask = sb("cmask", [P, 384], bf16)
        mmask = sb("mmask", [P, 384], bf16)
        gmask = sb("gmask", [P, 384], i8)
        chunk_start = sb("chunk_start", [P, 2 * T], bf16)
        sel4 = sb("sel4", [4, 4, P])
        ones = sb("ones", [P, 2])
        gw = sb("gw", [16, T])
        st = sb("st", [P, 128])
        cnt_i = sb("cnt_i", [P, 1], i32)

        at = [0]

        def piece(n):
            at[0] += n
            assert at[0] <= late.shape[1]
            return late[:, at[0] - n:at[0]]

        zqk_flat = piece(8 * (T + 3))
        zqk = zqk_flat[:, 0:NT * 2 * MIX].rearrange("p (t n) -> p t n", t=NT)
        conv_in = zqk_flat.rearrange("p (m n) -> p m n", m=8)
        qkT_flat = piece(8 * T)
        qkT = qkT_flat.rearrange("p (m n) -> p m n", m=8)
        g_att = qkT_flat[:, 0:1536].rearrange("p (h n) -> p h n", h=4)
        vm = piece(NT * MIX).rearrange("p (t n) -> p t n", t=NT)
        vg = piece(NT * MIX).rearrange("p (t n) -> p t n", t=NT)
        vl = piece(NT * MIX).rearrange("p (t n) -> p t n", t=NT)
        gr = piece(NT * MIX).rearrange("p (t n) -> p t n", t=NT)
        lo = piece(NT * MIX).rearrange("p (t n) -> p t n", t=NT)
        gqk = piece(4 * T).rearrange("p (m n) -> p m n", m=4)
        mqk_flat = piece(8 * T)
        mqk = mqk_flat.rearrange("p (m n) -> p m n", m=8)
        gates_flat = piece(2 * NT * W)
        gates = gates_flat.rearrange("p (a t n) -> p a t n", a=2, t=NT)
        pT = gates_flat[:, 0:1536].rearrange("p (h n) -> p h n", h=4)
        rows = piece(7 * T).rearrange("p (m n) -> p m n", m=7)
        rope = piece(2 * NT * 8).rearrange("p (a t n) -> p a t n", a=2, t=NT)
        zs = piece(NT * 24).rearrange("p (t n) -> p t n", t=NT)
        aT, iT, fT, cumf, gl, rmax, fls = (rows[:, i] for i in range(7))
        sc = tmp[:, :].rearrange("p (g h n) -> p g h n", g=2, h=4)
        rt = tmp[:, 0:1024].rearrange("p (m t h n) -> p m t h n", m=4, t=NT, h=16)
        gA, gB, gC, gE = (tmp[:, i * 512:(i + 1) * 512] for i in range(4))
        gx = tmp[:, 2048:2048 + 384].rearrange("p (m n) -> p m n", m=2)
        mE = tmp[:, 0:1536].rearrange("p (h n) -> p h n", h=4)
        mW = tmp[:, 1536:3072].rearrange("p (h n) -> p h n", h=4)
        ws_raw = tmp[:, 0:KT * 24]
        silu_g = ytok[:, 0, :].rearrange("p (t n) -> p t n", t=NT)
        hid = ytok[:, 1, :].rearrange("p (t n) -> p t n", t=NT)
        ysb = tmp[:, 0:D]
        fin_g = tmp[:, D:2 * D]
        ffn_g = tmp[:, 2 * D:3 * D]
        bflat = bias[:, :, :].rearrange("p a n -> p (a n)")
        sel = bflat[:, 0:256].rearrange("p (t n) -> p t n", t=NT)
        selg = bflat[:, 256:512].rearrange("p (t n) -> p t n", t=NT)
        selT = bflat[:, 512:768]
        iota = bflat[:, 768:896]
        tri = bflat[:, 896:1024]
        allones = bflat[:, 1024:1152]
        iota_i = bflat[:, 1152:1280].bitcast(i32)
        pos = bflat[:, 1280:1280 + 34].rearrange("p (t n) -> p t n", t=NT)
        gmat = bflat[:, 1320:1320 + 34].rearrange("p (t n) -> p t n", t=NT)
        ind = bflat[:, 1360:1376].rearrange("p (t n) -> p t n", t=NT)
        lg = bflat[:, 1376:1392].rearrange("p (t n) -> p t n", t=NT)
        m8 = bflat[:, 1392:1408].rearrange("p (t n) -> p t n", t=NT)
        idx = bflat[:, 1408:1424].bitcast(u32).rearrange("p (t n) -> p t n", t=NT)
        idf = bflat[:, 1424:1440].rearrange("p (t n) -> p t n", t=NT)
        oh = bflat[:, 1440:1472].rearrange("p (a t n) -> p a t n", a=2, t=NT)
        rbias = bflat[:, 1480:1488]
        g12 = bflat[:, 1488:1496].rearrange("p (t n) -> p t n", t=NT)
        ss, var, y0, nt0, rstd = (st[:, 2 * i:2 * i + 2] for i in range(5))
        mx = st[:, 16:32].rearrange("p (g t h) -> p g t h", g=2, t=NT)
        sums = st[:, 32:48].rearrange("p (g t h) -> p g t h", g=2, t=NT)
        gss, gvar, gy0, gn0, grs = (st[:, 48 + 8 * i:56 + 8 * i] for i in range(5))
        lcol = st[:, 88:104]
        lden, lrin = st[:, 104:112], st[:, 112:120]

        def slot_raw(n, moe):
            s = n % (RE if moe else RM)
            return raw_m[:, s, :] if s < RM else late[:, (s - RM) * CK:(s - RM + 1) * CK]

        ps = ctx.enter_context(nc.psum_tensor("ps", [P, 8, W], f32))

        raw_in = [sem(f"raw_in{i}") for i in range(RM)]
        moe_in = [sem(f"moe_in{i}") for i in range(RE)]
        hi_ready = sem("w_hi_ready")
        lo_ready = sem("w_lo_ready")
        w_used = sem("w_used")
        full = [sem(f"bank_full{i}") for i in range(8)]
        drained = [sem(f"bank_drained{i}") for i in range(8)]
        bias_in = [sem(f"bias_in{i}") for i in range(3)]
        c_in = sem("columns_in")
        c2_in = sem("constants_in")
        x_in = sem("x_in")
        ws_in = sem("small_weights_in")
        fg_in = sem("norm_gains_in")
        consts = sem("masks_built")
        moe_consts = sem("moe_tables_built")
        pads = sem("conv_pads_zeroed")
        act_seq = sem("act_seq")
        dve_seq = sem("dve_seq")
        out_done = sem("out_done")
        stat = sem("row_stats_ready")
        statv = sem("row_stats_scaled")
        xn_ready = sem("xn_ready")
        hi_part = sem("hi_part_ready")
        ws_hi_ready = sem("small_hi_ready")
        ws_ready = sem("small_ready")
        rope_done = sem("rope_done")
        p_ready = sem("probs_ready")
        y_ready = sem("y_gla_mlstm_ready")
        lsg2 = sem("log_sigmoid_done")
        gla_cum = sem("gla_cumsum")
        gla_exp = sem("gla_exps")
        gla_ops = sem("gla_operands")
        rows_ready = sem("mlstm_rows_ready")
        floors = sem("mlstm_floors")
        mEr = sem("mlstm_decays")
        conv0 = sem("conv_first_tap")
        conv3 = sem("conv_taps_done")
        mqk_ready = sem("mqk_ready")
        gate_ready = sem("gates_ready")
        sub_ready = sem("scores_shifted")
        conv_out = sem("conv_inputs_ready")
        gstat = sem("gla_stats_ready")
        gstatv = sem("gla_stats_scaled")
        GATES = {"gr": 1, "lo": 2}
        for b in range(3):
            GATES[f"g{b}"] = 4 + 4 * b
            GATES[f"g{b}'"] = 6 + 4 * b
        NG = 14
        merged_ready = sem("merged_ready")
        silu_ready = sem("silu_ready")
        router_e = sem("router_exp")
        router_d2 = sem("router_gap")
        ind_ready = sem("picks_ready")
        pos_ready = sem("positions_ready")
        sel_ready = sem("selection_ready")
        zeroed = sem("expert_rows_zeroed")

        block = ctx.enter_context(nc.Block())

        def last_use(n):
            kind, v = USED[n]
            if kind == "w":
                return w_used, v
            b, k = FILL[v]
            return full[b], k + 1

        def moe_last_use(pas, e, j):
            kind, v = EUSED[j % FFC]
            back = -1 if j < 0 else 0
            if kind == "w":
                return w_used, MOE_USED0 + (pas * E + back) * EU + v + e * EU
            b, k = EXPERT[v]
            return full[b], PASS_FILL[pas][b] + PRO.get(b, 0) + k + 1 + back * nexp[b] + e * nexp[b]

        def moe_fill(pas, e, tag, i):
            b, k = EXPERT[tag, i]
            return b, PASS_FILL[pas][b] + PRO.get(b, 0) + k + e * nexp[b]

        @block.sync
        def _(sp):
            for t in range(NT):
                sp.dma_start(xt[:, t, :], x[t * P:(t + 1) * P, :]).then_inc(x_in, 16)
            sp.dma_start(cols[:, :, :], cols_d.rearrange("l p n -> p l n")).then_inc(c_in, 16)

            def source(l, n):
                name, o = UNITS[n // 2]
                c = n % 2
                if name[:2] == "up":
                    return w_up[o][l, 2 * c * P:2 * (c + 1) * P, :].rearrange("(k p) n -> p k n", p=P)
                m = w_o if name[:2] == "wo" else w_in
                return m[l, 4 * c * P:4 * (c + 1) * P, o:o + W].rearrange("(k p) n -> p k n", p=P)

            def load_ff(dst, g, u, d, kind, i, c, done):
                if kind == "gu":
                    v = dst.rearrange("p (k n) -> p k n", k=4)
                    for half, m in enumerate((g, u)):
                        sp.dma_start(v[:, :, half * 256:(half + 1) * 256],
                                     m(slice(4 * c * P, 4 * (c + 1) * P), slice(i * 256, (i + 1) * 256))
                                     .rearrange("(k p) n -> p k n", p=P)).then_inc(done, 16)
                else:
                    v = dst.rearrange("p (k n) -> p k n", k=2)
                    for k in range(2):
                        sp.dma_start(v[:, k, :], d(slice(i * 256 + k * P, i * 256 + (k + 1) * P), slice(0, D)))\
                            .then_inc(done, 16)

            for l in range(L):
                for n in range(2 * NU):
                    g = LAYER_BASE[l] + n
                    if g >= RM:
                        sp.wait_ge(lo_ready, g - RM + 1)
                    s = source(l, n)
                    k = s.shape[1]
                    v = slot_raw(g, False).rearrange("p (k n) -> p k n", k=k)
                    for h in range(2):
                        sp.dma_start(v[:, h * k // 2:(h + 1) * k // 2, :], s[:, h * k // 2:(h + 1) * k // 2, :])\
                            .then_inc(raw_in[g % RM], 16)
                if l == 0:
                    for n, (kind, i, c) in enumerate(FF):
                        g = 2 * NU + n
                        sp.wait_ge(lo_ready, g - RM + 1)
                        load_ff(slot_raw(g, False), lambda r, q: ffn_gate[r, q], lambda r, q: ffn_up[r, q],
                                lambda r, q: ffn_down[r, q], kind, i, c, raw_in[g % RM])
            sp.wait_ge(lo_ready, MOE_BASE)
            sp.wait_ge(merged_ready, L * NT)

            def moe_loads(pas):
                with sp.Fori(0, E) as e:
                    for j, (kind, i, c) in enumerate(FF):
                        sp.wait_ge(lo_ready, e * FFC + (MOE_BASE + pas * E * FFC + j - RE + 1))

                        def view(m):
                            return lambda r, q: m[bass.ds(e, 1), r, q].rearrange("a r q -> (a r) q")
                        load_ff(slot_raw(j, True), view(moe_gate), view(moe_up), view(moe_down), kind, i, c,
                                moe_in[j % RE])

            moe_loads(0)
            sp.wait_ge(pos_ready, 1)
            many = sp.value_load(cnt_i[0:1, 0:1], min_val=0, max_val=T)
            with sp.If(many > P):
                moe_loads(1)
            sp.wait_ge(xn_ready, (2 * L + 1) * NT)
            for t in range(NT):
                sp.dma_start(out[t * P:(t + 1) * P, :], xn[:, t, :]).then_inc(out_done, 16)
            sp.wait_ge(out_done, 16 * NT)

        @block.gpsimd
        def _(pool):
            pool.dma_start(bsm[:, :, :], b_small_d.partition_broadcast(P)).then_inc(c2_in, 16)
            pool.dma_start(rope[:, :, :, :], rope_d).then_inc(c2_in, 16)
            built = 0

            def fence(ins):
                nonlocal built
                ins.then_inc(consts, 1)
                built += 1
                pool.wait_ge(consts, built)

            fence(nc.gpsimd.memset(ident[:, :], 0.0))
            fence(nc.gpsimd.affine_select(out=ident[:, :], in_=ident[:, :], compare_op=ALU.not_equal, fill=1.0,
                                          base=0, pattern=[[-1, P]], channel_multiplier=1))
            nc.gpsimd.memset(ones[:, :], 1.0)
            nc.gpsimd.memset(ones_row[:, :], 1.0)
            nc.gpsimd.memset(cmask[:, :], 0.0)
            nc.gpsimd.memset(mmask[:, :], 1.0)
            nc.gpsimd.memset(gmask[:, :], 1)
            nc.gpsimd.memset(chunk_start[:, :], 1.0)
            fence(nc.gpsimd.memset(sel4[:, :, :], 0.0))
            nc.gpsimd.memset(chunk_start[:, 0:2 * T:CH], 0.0)
            v = cmask[:, P:3 * P].rearrange("p (a n) -> p a n", a=2)
            nc.gpsimd.affine_select(out=v, in_=v, compare_op=ALU.is_ge, fill=-1e30, base=0,
                                    pattern=[[0, 2], [-1, P]], channel_multiplier=1)
            for m in (mmask, gmask):
                for c in (0, 2 * P):
                    v = m[:, c:c + P]
                    nc.gpsimd.affine_select(out=v, in_=v, compare_op=ALU.is_ge, fill=0.0, base=0,
                                            pattern=[[1, P]], channel_multiplier=-1)
            fence(nc.gpsimd.affine_select(out=sel4[:, :, :], in_=sel4[:, :, :], compare_op=ALU.not_equal, fill=1.0,
                                          base=0, pattern=[[1, 4], [0, P]], channel_multiplier=-1))
            n = 0
            for l in range(L):
                if l:
                    pool.wait_ge(full[FILL[l - 1, "acc", 3][0]], FILL[l - 1, "acc", 3][1] + 1)
                pool.dma_start(ws_raw, w_small_d[l]).then_inc(ws_in, 16)
                pool.dma_start(gw[0:16, :], gate_w[l]).then_inc(ws_in, 16)
                for name, o in UNITS:
                    if name not in BIASED:
                        continue
                    if n >= 3:
                        pl, pname = divmod(n - 3, len(BIASED))
                        b, k = FILL[pl, BIASED[pname], 1]
                        pool.wait_ge(drained[b], k + 1)
                    pool.dma_start(bias[:, n % 3, :], b_in[l, o:o + W].partition_broadcast(P))\
                        .then_inc(bias_in[n % 3], 16)
                    n += 1
                    if name == "mv":
                        b, k = FILL[l, "qkT", 3]
                        pool.wait_ge(full[b], k + 1)
                        nc.gpsimd.memset(conv_in[:, :, 0:3], 0.0).then_inc(pads, 1)
                    if name == "gr":
                        b, k = FILL[l, "s1", 3]
                        pool.wait_ge(full[b], k + 1)
                        nc.gpsimd.memset(g_att, 0.0).then_inc(pads, 1)
            b, k = FILL[L - 1, "g2'", 1]
            pool.wait_ge(drained[b], k + 1)
            made = 0

            def fence2(ins):
                nonlocal made
                ins.then_inc(moe_consts, 1)
                made += 1
                pool.wait_ge(moe_consts, made)

            nc.gpsimd.memset(allones, 1.0)
            nc.gpsimd.iota(iota_i, pattern=[[1, P]], base=0, channel_multiplier=0)
            nc.gpsimd.memset(pos[:, :, 16:17], -1.0)
            nc.gpsimd.memset(gmat[:, :, 16:17], 0.0)
            fence2(nc.gpsimd.memset(tri, 1.0))
            fence2(nc.gpsimd.affine_select(out=tri, in_=tri, compare_op=ALU.is_gt, fill=0.0, base=0,
                                           pattern=[[1, P]], channel_multiplier=-1))
            pool.dma_start(rbias, router_b.partition_broadcast(P)).then_inc(fg_in, 16)
            pool.wait_ge(y_ready, 2 * L * NT)
            pool.dma_start(ws_raw[:, 0:KT * E], router_d).then_inc(ws_in, 16)
            pool.dma_start(fin_g, final_g.partition_broadcast(P)).then_inc(fg_in, 16)
            pool.dma_start(ffn_g, ffn_norm_g[L - 1].partition_broadcast(P)).then_inc(fg_in, 16)
            pool.wait_ge(fg_in, 48)

        @block.tensor
        def _(pe):
            mm = nc.tensor.matmul
            for_3 = ((0, 0), (0, 1), (1, 0))
            hT, yT, ws, wsp = (hT_hi, hT_lo), (yT_hi, yT_lo), (ws_hi, ws_lo), (w_hi, w_lo)
            hT_count = [0]

            def claim(l, tag, i=0):
                b, k = FILL[l, tag, i]
                if k:
                    pe.wait_ge(drained[b], k)
                return b

            def done(ins, l, tag, i=0):
                ins.then_inc(full[FILL[l, tag, i][0]], 1)

            def await_drained(l, tag, i=0):
                b, k = FILL[l, tag, i]
                pe.wait_ge(drained[b], k + 1)

            def transposes_of_xn(l, tag):
                banks = [claim(l, tag, i) for i in range(4)]
                for t in range(NT):
                    for k in range(KT):
                        ins = nc.tensor.transpose(ps[:, banks[k // 2], (k % 2) * T + t * P:(k % 2) * T + (t + 1) * P],
                                                  xn[:, t, k * P:(k + 1) * P], ident[:, :])
                        if t == NT - 1 and k % 2:
                            done(ins, l, tag, k // 2)

            def unit(l, name):
                n0 = LAYER_BASE[l] + 2 * UIDX[name]
                nb = 4 if name[:2] == "up" else 2
                banks = [FILL[l, name, i] for i in range(nb)]
                for c in range(2):
                    n = n0 + c
                    pe.wait_ge(lo_ready, n + 1)
                    s = n % RS
                    if name in FEATURE_MAJOR:
                        for i in range(2):
                            if c == 0:
                                claim(l, name, i)
                            for kk in range(4):
                                k = 4 * c + kk
                                for m in (2 * i, 2 * i + 1):
                                    for pa, (a, b) in enumerate(for_3):
                                        ins = mm(ps[:, banks[i][0], (m % 2) * T:(m % 2 + 1) * T],
                                                 wsp[a][:, s, kk * W + m * P:kk * W + (m + 1) * P], hT[b][:, k, :],
                                                 start=(k == 0 and m % 2 == 0 and pa == 0),
                                                 stop=(k == KT - 1 and m % 2 == 1 and pa == 2), skip_group_check=True)
                            if c:
                                done(ins, l, name, i)
                    elif nb == 2:
                        for t in range(NT):
                            if c == 0:
                                claim(l, name, t)
                            for kk in range(4):
                                k = 4 * c + kk
                                for pa, (a, b) in enumerate(for_3):
                                    ins = mm(ps[:, banks[t][0], :], hT[a][:, k, t * P:(t + 1) * P],
                                             wsp[b][:, s, kk * W:(kk + 1) * W],
                                             start=(k == 0 and pa == 0), stop=(k == KT - 1 and pa == 2))
                            if c:
                                done(ins, l, name, t)
                    else:
                        for t in range(NT):
                            for h in range(2):
                                if c == 0:
                                    claim(l, name, 2 * t + h)
                                for kk in range(2):
                                    k = 2 * c + kk
                                    for pa, (a, b) in enumerate(for_3):
                                        ins = mm(ps[:, banks[2 * t + h][0], :], yT[a][:, k, t * P:(t + 1) * P],
                                                 wsp[b][:, s, kk * D + h * W:kk * D + (h + 1) * W],
                                                 start=(k == 0 and pa == 0), stop=(k == 3 and pa == 2))
                                if c:
                                    done(ins, l, name, 2 * t + h)
                    if c == 0:
                        ins.then_inc(w_used, 1)

            def y_transposes(l, br):
                if br:
                    pe.wait_ge(y_ready, (2 * l + br) * NT)
                else:
                    await_drained(l, "pv1", 0)
                    await_drained(l, "pv1", 1)
                for i in range(2):
                    b = claim(l, f"yT{br}", i)
                    for m in range(2):
                        for t in range(NT):
                            ins = nc.tensor.transpose(ps[:, b, m * T + t * P:m * T + (t + 1) * P],
                                                      ytok[:, t, (2 * i + m) * P:(2 * i + m + 1) * P], ident[:, :])
                    done(ins, l, f"yT{br}", i)

            def scores(l, g):
                for hh in range(4):
                    h = 4 * g + hh
                    b = claim(l, f"s{g}", hh)
                    p0 = HD * (h % 2)
                    q, k = qkT[p0:p0 + HD, h // 2, :], qkT[p0:p0 + HD, 4 + h // 2, :]
                    mm(ps[:, b, 0:T], q[:, P:2 * P], k, start=True, stop=True)
                    done(mm(ps[:, b, T:T + P], q[:, 0:P], k[:, 0:P], start=True, stop=True), l, f"s{g}", hh)

            def prob_transposes(l, g):
                pe.wait_ge(p_ready, 2 * l + g + 1)
                for hh in range(4):
                    b = claim(l, f"pT{g}", hh)
                    for j in range(3):
                        ins = nc.tensor.transpose(ps[:, b, j * P:(j + 1) * P], sc[:, g, hh, j * P:(j + 1) * P],
                                                  ident[:, :])
                    done(ins, l, f"pT{g}", hh)

            def prob_values(l, g):
                for hh in range(4):
                    await_drained(l, f"pT{g}", hh)
                b0, b1 = claim(l, f"pv{g}", 0), claim(l, f"pv{g}", 1)
                for hh in range(4):
                    h = 4 * g + hh
                    ins = mm(ps[:, b0, hh * HD:(hh + 1) * HD], pT[:, hh, 2 * P:3 * P], vm[:, 0, h * HD:(h + 1) * HD],
                             start=True, stop=True)
                done(ins, l, f"pv{g}", 0)
                for hh in range(4):
                    h = 4 * g + hh
                    for j in range(2):
                        ins = mm(ps[:, b1, hh * HD:(hh + 1) * HD], pT[:, hh, j * P:(j + 1) * P],
                                 vm[:, j, h * HD:(h + 1) * HD], start=(j == 0), stop=(j == 1))
                done(ins, l, f"pv{g}", 1)

            def gla_scores(l):
                pe.wait_ge(gla_ops, l + 1)
                ki, ke = gB.rearrange("p (m n) -> p m n", m=2), gE.rearrange("p (m n) -> p m n", m=2)
                for h in range(4):
                    b = claim(l, "gs", h)
                    p0, m = GD * (h % 2), h // 2

                    def block_(c, col, lhs, rhs):
                        q0 = CH * (c % 2)
                        return mm(ps[q0:q0 + CH, b, col:col + rhs.shape[1]], lhs[p0:p0 + GD, m, c * CH:(c + 1) * CH],
                                  rhs, start=True, stop=True)
                    qd = gqk[p0:p0 + GD, m, :]
                    for c in range(4):
                        lo_col = 0 if c < 2 else T
                        q_lo = 0 if c < 2 else P
                        if c % 2:
                            block_(c, lo_col, ke, qd[:, q_lo:q_lo + CH])
                        ins = block_(c, lo_col + CH * (c % 2), ki, qd[:, c * CH:(c + 1) * CH])
                        if c < 3:
                            ins = block_(c, lo_col + CH * (c % 2) + CH, ke, qd[:, (c + 1) * CH:(c + 2) * CH])
                        if c == 0:
                            ins = block_(c, P, ke, gx[p0:p0 + GD, m, 0:2 * CH])
                        if c == 1:
                            ins = block_(c, 3 * CH, ke, gx[p0:p0 + GD, m, 2 * CH:3 * CH])
                    done(ins, l, "gs", h)

            def att_values(l, tag, att, v):
                b0, b1 = claim(l, tag, 0), claim(l, tag, 1)
                for h in range(4):
                    ins = mm(ps[:, b0, h * P:(h + 1) * P], att[:, h, 0:P], v[:, 0, h * P:(h + 1) * P],
                             start=True, stop=True)
                done(ins, l, tag, 0)
                for h in range(4):
                    mm(ps[:, b1, h * P:(h + 1) * P], att[:, h, P:2 * P], v[:, 0, h * P:(h + 1) * P],
                       start=True, stop=False)
                    ins = mm(ps[:, b1, h * P:(h + 1) * P], att[:, h, 2 * P:3 * P], v[:, 1, h * P:(h + 1) * P],
                             start=False, stop=True)
                done(ins, l, tag, 1)

            pe.wait_ge(consts, 4)
            for l in range(L):
                pe.wait_ge(xn_ready, (2 * l + 1) * NT)
                transposes_of_xn(l, "norm")
                for i in range(4):
                    await_drained(l, "norm", i)
                unit(l, "mq")
                unit(l, "mk")
                pe.wait_ge(ws_ready, l + 1)
                b = claim(l, "small")
                for t in range(NT):
                    for k in range(KT):
                        for pa, (a, c) in enumerate(for_3):
                            ins = mm(ps[:, b, t * 24:(t + 1) * 24], hT[a][:, k, t * P:(t + 1) * P],
                                     ws[c][:, k * 24:(k + 1) * 24], start=(k == 0 and pa == 0),
                                     stop=(k == KT - 1 and pa == 2))
                done(ins, l, "small")
                unit(l, "mv")
                await_drained(l, "small")
                b, b2 = claim(l, "smallT", 0), claim(l, "smallT", 1)
                for t in range(NT):
                    nc.tensor.transpose(ps[0:16, b, t * P:(t + 1) * P], zs[:, t, 0:16], ident[:, :])
                    ins = nc.tensor.transpose(ps[0:4, b, T + t * P:T + (t + 1) * P], zs[:, t, 16:20], ident[:, :])
                done(ins, l, "smallT", 0)
                for t in range(NT):
                    ins = nc.tensor.transpose(ps[0:4, b2, t * P:(t + 1) * P], zs[:, t, 20:24], ident[:, :])
                done(ins, l, "smallT", 1)
                pe.wait_ge(rope_done, l + 1)
                for i in range(4):
                    b = claim(l, "qkT", i)
                    for m in range(2):
                        for t in range(NT):
                            ins = nc.tensor.transpose(ps[:, b, m * T + t * P:m * T + (t + 1) * P],
                                                      zqk[:, t, (2 * i + m) * P:(2 * i + m + 1) * P], ident[:, :])
                    done(ins, l, "qkT", i)
                unit(l, "gqk")
                unit(l, "gv")
                for i in range(4):
                    await_drained(l, "qkT", i)
                scores(l, 0)
                unit(l, "gr")
                scores(l, 1)
                unit(l, "lq")
                await_drained(l, "mv", 1)
                prob_transposes(l, 0)
                prob_values(l, 0)
                unit(l, "lk")
                prob_transposes(l, 1)
                prob_values(l, 1)
                b = claim(l, "ga")
                pe.wait_ge(ws_in, 32 * (l + 1))
                await_drained(l, "smallT", 0)
                for m in range(2):
                    ins = mm(ps[:, b, m * T:(m + 1) * T], gw[0:16, m * P:(m + 1) * P], aT[0:16, :],
                             start=True, stop=True)
                done(ins, l, "ga")
                unit(l, "lv")
                y_transposes(l, 0)
                unit(l, "lo")
                gla_scores(l)
                unit(l, "g0")
                for i in range(4):
                    await_drained(l, "gs", i)
                await_drained(l, "gv", 1)
                att_values(l, "go", g_att, vg)
                unit(l, "g0'")
                pe.wait_ge(rows_ready, l + 1)
                pe.wait_ge(floors, l + 1)
                for i in range(2):
                    b = claim(l, "mb", i)
                    for hh in range(2):
                        ins = mm(ps[:, b, hh * T:(hh + 1) * T], sel4[0:4, 2 * i + hh, :], rmax[0:4, :],
                                 start=True, stop=True)
                    done(ins, l, "mb", i)
                b = claim(l, "mb", 2)
                for i, r in enumerate((gl, fls)):
                    for t in range(NT):
                        ins = nc.tensor.transpose(ps[:, b, 8 * i + 4 * t:8 * i + 4 * t + 4],
                                                  r[0:4, t * P:(t + 1) * P], ident[0:4, 0:4])
                done(ins, l, "mb", 2)
                for i in range(2):
                    await_drained(l, "yT0", i)
                unit(l, "up0")
                y_transposes(l, 1)
                pe.wait_ge(mqk_ready, 2 * (l + 1))
                for h in range(4):
                    b = claim(l, "ms", h)
                    mm(ps[:, b, 0:T], mqk[:, 4 + h, 0:P], mqk[:, h, :], start=True, stop=True)
                    done(mm(ps[:, b, T:T + P], mqk[:, 4 + h, P:2 * P], mqk[:, h, P:2 * P], start=True, stop=True),
                         l, "ms", h)
                unit(l, "g1")
                unit(l, "g1'")
                for i in range(4):
                    await_drained(l, "ms", i)
                await_drained(l, "lv", 1)
                att_values(l, "mo", mW, vl)
                b = claim(l, "mo", 2)
                for h in range(4):
                    mm(ps[:, b, h:h + 1], mW[:, h, 0:P], ones[:, 0:1], start=True, stop=True)
                    mm(ps[:, b, 4 + h:5 + h], mW[:, h, P:2 * P], ones[:, 0:1], start=True, stop=False)
                    ins = mm(ps[:, b, 4 + h:5 + h], mW[:, h, 2 * P:3 * P], ones[:, 0:1], start=False, stop=True)
                done(ins, l, "mo", 2)
                for i in range(2):
                    await_drained(l, "yT1", i)
                unit(l, "up1")
                y_transposes(l, 2)
                unit(l, "g2")
                unit(l, "g2'")
                for i in range(2):
                    await_drained(l, "yT2", i)
                unit(l, "up2")
                pe.wait_ge(merged_ready, (l + 1) * NT)
                transposes_of_xn(l, "mgT")
                for i in range(4):
                    await_drained(l, "mgT", i)
                unit(l, "wo")
                unit(l, "wo'")
                pe.wait_ge(xn_ready, (2 * l + 2) * NT)
                transposes_of_xn(l, "fnorm")
                for i in range(4):
                    await_drained(l, "fnorm", i)
                if l == 0:
                    def hidden_T(i):
                        for t in range(NT):
                            await_drained(0, f"gu{i}", t)
                        b = claim(0, f"hT{i}")
                        for m in range(2):
                            for t in range(NT):
                                ins = nc.tensor.transpose(ps[:, b, m * T + t * P:m * T + (t + 1) * P],
                                                          hid[:, t, m * P:(m + 1) * P], ident[:, :])
                        done(ins, 0, f"hT{i}")

                    for n, (kind, i, c) in enumerate(FF):
                        g = 2 * NU + n
                        if kind == "dn":
                            await_drained(0, f"hT{i}")
                        pe.wait_ge(lo_ready, g + 1)
                        s = g % RS
                        for t in range(NT):
                            if kind == "gu":
                                b = claim(0, f"gu{i}", t) if c == 0 else FILL[0, f"gu{i}", t][0]
                                for kk in range(4):
                                    k = 4 * c + kk
                                    for pa, (a, r) in enumerate(for_3):
                                        ins = mm(ps[:, b, :], hT[a][:, k, t * P:(t + 1) * P],
                                                 wsp[r][:, s, kk * W:(kk + 1) * W],
                                                 start=(k == 0 and pa == 0), stop=(k == KT - 1 and pa == 2))
                                if c:
                                    done(ins, 0, f"gu{i}", t)
                                continue
                            for h in range(2):
                                b = claim(0, "acc", 2 * t + h) if i == 0 else FILL[0, "acc", 2 * t + h][0]
                                for kk in range(2):
                                    for pa, (a, r) in enumerate(for_3):
                                        ins = mm(ps[:, b, :], yT[a][:, 2 * (i % 2) + kk, t * P:(t + 1) * P],
                                                 wsp[r][:, s, kk * D + h * W:kk * D + (h + 1) * W],
                                                 start=(i == 0 and kk == 0 and pa == 0),
                                                 stop=(i == NF - 1 and kk == 1 and pa == 2))
                                if i == NF - 1:
                                    done(ins, 0, "acc", 2 * t + h)
                        if USED[g][0] == "w":
                            ins.then_inc(w_used, 1)
                        if kind == "dn" and i + 1 < NF or kind == "gu" and c == 1 and i == 0:
                            hidden_T(i + 1 if kind == "dn" else 0)

            pe.wait_ge(ws_ready, L + 1)
            b = claim(1, "logits")
            for t in range(NT):
                for k in range(KT):
                    for pa, (a, c) in enumerate(for_3):
                        ins = mm(ps[:, b, t * E:(t + 1) * E], hT[a][:, k, t * P:(t + 1) * P],
                                 ws[c][:, k * E:(k + 1) * E], start=(k == 0 and pa == 0),
                                 stop=(k == KT - 1 and pa == 2))
            done(ins, 1, "logits")
            pe.wait_ge(moe_consts, 2)
            pe.wait_ge(ind_ready, 1)
            b = claim(1, "rank")
            mm(ps[:, b, 0:E], tri, ind[:, 0, :], start=True, stop=True)
            mm(ps[:, b, E:2 * E], allones, ind[:, 0, :], start=True, stop=False)
            mm(ps[:, b, E:2 * E], tri, ind[:, 1, :], start=False, stop=True)
            mm(ps[:, b, 2 * E:3 * E], allones, ind[:, 0, :], start=True, stop=False)
            done(mm(ps[:, b, 2 * E:3 * E], allones, ind[:, 1, :], start=False, stop=True), 1, "rank")

            def gather(banks, waits):
                for i in range(2):
                    pe.wait_ge(drained[banks[i]], waits[i])
                    for kk in range(4):
                        k = 4 * i + kk
                        for t in range(NT):
                            ins = mm(ps[:, banks[i], kk * P:(kk + 1) * P], xn[:, t, k * P:(k + 1) * P], sel[:, t, :],
                                     start=(t == 0), stop=(t == NT - 1))
                    ins.then_inc(full[banks[i]], 1)

            def scatter(fill):
                for t in range(NT):
                    for h in range(2):
                        b, k = fill(t, h)
                        pe.wait_ge(drained[b], k)
                        mm(ps[:, b, :], selT[:, t * P:(t + 1) * P], ysb[:, h * W:(h + 1) * W],
                           start=True, stop=True).then_inc(full[b], 1)

            def moe_pass(pas):
                base = PASS_FILL[pas]
                pe.wait_ge(zeroed, pas + 1)
                pe.wait_ge(sel_ready, pas * (E + 1) + 1)
                gather((6, 7), (base[6], base[7]))
                with pe.Fori(0, E) as e:
                    def bank(tag, i=0):
                        b, k = moe_fill(pas, e, tag, i)
                        pe.wait_ge(drained[b], k)
                        return b

                    def hidden_T(i):
                        b, k = moe_fill(pas, e, f"gu{i}", 0)
                        pe.wait_ge(drained[b], k + 1)
                        b = bank(f"hT{i}")
                        for m in range(2):
                            ins = nc.tensor.transpose(ps[:, b, m * P:(m + 1) * P], hid[:, i % 2, m * P:(m + 1) * P],
                                                      ident[:, :])
                        ins.then_inc(full[b], 1)

                    for n, (kind, i, c) in enumerate(FF):
                        if n == 0:
                            for q in (6, 7):
                                pe.wait_ge(drained[q], base[q] + PRO[q] + e * nexp[q])
                        if kind == "dn":
                            b, k = moe_fill(pas, e, f"hT{i}", 0)
                            pe.wait_ge(drained[b], k + 1)
                        if n == FFC - 1:
                            pe.wait_ge(sel_ready, pas * (E + 1) + 2 + e)
                            fb = [moe_fill(pas, e, "gather", q) for q in range(2)]
                            gather([f[0] for f in fb], [f[1] for f in fb])
                        pe.wait_ge(lo_ready, e * FFC + (MOE_BASE + pas * E * FFC + n + 1))
                        s = n % RS
                        if kind == "gu":
                            b = bank(f"gu{i}") if c == 0 else EXPERT[f"gu{i}", 0][0]
                            for kk in range(4):
                                k = 4 * c + kk
                                for pa, (a, r) in enumerate(for_3):
                                    ins = mm(ps[:, b, :], hT[a][:, k, 0:P], wsp[r][:, s, kk * W:(kk + 1) * W],
                                             start=(k == 0 and pa == 0), stop=(k == KT - 1 and pa == 2))
                            if c:
                                ins.then_inc(full[b], 1)
                        else:
                            for h in range(2):
                                b = bank("acc", h) if i == 0 else EXPERT["acc", h][0]
                                for kk in range(2):
                                    for pa, (a, r) in enumerate(for_3):
                                        ins = mm(ps[:, b, :], yT[a][:, 2 * (i % 2) + kk, 0:P],
                                                 wsp[r][:, s, kk * D + h * W:kk * D + (h + 1) * W],
                                                 start=(i == 0 and kk == 0 and pa == 0),
                                                 stop=(i == NF - 1 and kk == 1 and pa == 2))
                                if i == NF - 1:
                                    ins.then_inc(full[b], 1)
                        if EUSED[n][0] == "w":
                            ins.then_inc(w_used, 1)
                        if kind == "gu" and c == 1 and i == 0:
                            for q in (3, 4, 5):
                                pe.wait_ge(drained[q], base[q] + e * nexp[q])
                            scatter(lambda t, h: moe_fill(pas, e, f"sc{t}", h))
                            hidden_T(0)
                        if kind == "dn" and i + 1 < NF:
                            hidden_T(i + 1)
                        if kind == "dn" and i == 4:
                            b = bank("selT")
                            for t in range(NT):
                                ins = nc.tensor.transpose(ps[:, b, t * P:(t + 1) * P], selg[:, t, :], ident[:, :])
                            ins.then_inc(full[b], 1)
                for q in (3, 4, 5):
                    pe.wait_ge(drained[q], base[q] + E * nexp[q])
                scatter(lambda t, h: (6 + h, base[6 + h] + PRO[6] + E * nexp[6 + h] + t))

            moe_pass(0)
            many = pe.value_load(cnt_i[0:1, 0:1], min_val=0, max_val=T)
            with pe.If(many > P):
                moe_pass(1)

        @block.scalar
        def _(act):
            copy, A = nc.scalar.copy, nc.scalar.activation
            seq, nsplit, norms = [0], [0], [0]

            def link(ins):
                seq[0] += 1
                ins.then_inc(act_seq, 1)
                act.wait_ge(act_seq, seq[0])

            def await_full(l, tag, i=0):
                b, k = FILL[l, tag, i]
                act.wait_ge(full[b], k + 1)
                return b

            def await_drained(l, tag, i=0):
                b, k = FILL[l, tag, i]
                act.wait_ge(drained[b], k + 1)

            def split_to(n):
                while nsplit[0] <= min(n, MOE_BASE - 1):
                    g = nsplit[0]
                    act.wait_ge(raw_in[g % RM], 32 * (g // RM + 1))
                    if g >= RS:
                        act.wait_ge(*last_use(g - RS))
                    copy(w_hi[:, g % RS, :], slot_raw(g, False)).then_inc(hi_ready, 1)
                    nsplit[0] += 1

            def ahead(l, name):
                split_to(LAYER_BASE[l] + 2 * UIDX[name] + 1 + 2)

            def norm_stats():
                for t in range(NT):
                    A(xn[:, t, :], xt[:, t, :], ACT.Square, accum_out=ss[:, t:t + 1]).then_inc(stat, 1)
                q = norms[0]
                norms[0] += 1
                act.wait_ge(statv, q + 1)
                link(A(nt0, var, ACT.Ln))
                A(y0, nt0, ACT.Exp, scale=-0.5).then_inc(stat, 1)

            def hi_of(l, tag, i, dst, gain=None):
                b = await_full(l, tag, i)
                if gain is None:
                    copy(dst[:, 2 * i:2 * i + 2, :], ps[:, b, :].rearrange("p (m n) -> p m n", m=2))\
                        .then_inc(hi_part, 1)
                    return
                for m in range(2):
                    k = 2 * i + m
                    ins = A(dst[:, k, :], ps[:, b, m * T:(m + 1) * T], ACT.Copy,
                            scale=cols[:, l, gain + k:gain + k + 1])
                ins.then_inc(hi_part, 1)

            def sigmoid_gates(l, name):
                b, h = int(name[1]), int(name.endswith("'"))
                for t in range(NT):
                    await_drained(l, name, t)
                    A(gates[:, h, t, :], gates[:, h, t, :], ACT.Sigmoid).then_inc(gate_ready, 1)

            def conv_head(l, name):
                u = 4 * (name == "lk")
                act.wait_ge(pads, 2 * l + 1)
                for i in range(2):
                    b = await_full(l, name, i)
                    for m in (2 * i, 2 * i + 1):
                        ins = A(conv_in[:, u + m, 3:3 + T], ps[:, b, (m % 2) * T:(m % 2 + 1) * T], ACT.Identity,
                                bias=cols[:, l, C_BL + u + m:C_BL + u + m + 1])
                    ins.then_inc(drained[b], 1)
                for i in range(2):
                    await_drained(l, name, i)
                for m in range(4):
                    c = C_CW + 4 * (u + m)
                    ins = A(mqk[:, u + m, :], conv_in[:, u + m, 0:T], ACT.Identity, scale=cols[:, l, c:c + 1],
                            bias=cols[:, l, C_CB + u + m:C_CB + u + m + 1])
                ins.then_inc(conv0, 1)

            act.wait_ge(x_in, 16 * NT)
            act.wait_ge(c_in, 16)
            for l in range(L):
                if l:
                    for i in range(4):
                        await_drained(l - 1, "acc", i)
                split_to(LAYER_BASE[l] + RS - 1)
                norm_stats()
                act.wait_ge(ws_in, 32 * (l + 1))
                copy(ws_hi[:, :], ws_raw).then_inc(ws_hi_ready, 1)
                for i in range(4):
                    hi_of(l, "norm", i, hT_hi, C_AG)
                ahead(l, "mq")
                ahead(l, "mk")
                ahead(l, "mv")
                for i in range(2):
                    b = await_full(l, "qkT", i)
                    copy(qkT[:, 2 * i:2 * i + 2, :], ps[:, b, :].rearrange("p (m n) -> p m n", m=2))\
                        .then_inc(drained[b], 1)
                ahead(l, "gqk")
                ahead(l, "gv")
                act.wait_ge(sub_ready, 2 * l + 1)
                A(sc[:, 0, :, :], sc[:, 0, :, :], ACT.Exp, scale=HD ** -0.5).then_inc(p_ready, 1)
                ahead(l, "gr")
                act.wait_ge(sub_ready, 2 * l + 2)
                A(sc[:, 1, :, :], sc[:, 1, :, :], ACT.Exp, scale=HD ** -0.5).then_inc(p_ready, 1)
                ahead(l, "lq")
                conv_head(l, "lq")

                def probs_out(g):
                    for hh in (0, 2):
                        b = await_full(l, f"pT{g}", hh)
                        copy(pT[:, hh, :], ps[:, b, 0:384]).then_inc(drained[b], 1)

                probs_out(0)
                ahead(l, "lk")
                conv_head(l, "lk")
                probs_out(1)
                await_drained(l, "ga")
                await_drained(l, "smallT", 1)
                A(gB, gA, ACT.Abs)
                link(A(cumf[0:4, :], fT[0:4, :], ACT.Abs))
                A(gB, gB, ACT.Exp, scale=-1.0)
                link(A(cumf[0:4, :], cumf[0:4, :], ACT.Exp, scale=-1.0))
                A(gB, gB, ACT.Ln, bias=1.0)
                A(cumf[0:4, :], cumf[0:4, :], ACT.Ln, bias=1.0).then_inc(lsg2, 1)
                ahead(l, "lv")
                act.wait_ge(rows_ready, l + 1)
                A(fls[0:4, :], fls[0:4, :], ACT.Exp, scale=-1.0).then_inc(floors, 1)
                act.wait_ge(gla_cum, l + 1)
                A(gA, gC, ACT.Exp, scale=1.0 / TAU)
                A(gB, gC, ACT.Exp, scale=-1.0 / TAU)
                A(gE, gE, ACT.Exp, scale=1.0 / TAU).then_inc(gla_exp, 1)
                for i in range(2):
                    hi_of(l, "yT0", i, yT_hi)
                ahead(l, "lo")
                for i in range(2):
                    await_drained(l, "gr", i)
                A(gr, gr, ACT.Silu).then_inc(gate_ready, 1)
                for u in range(2):
                    act.wait_ge(conv3, 2 * l + u + 1)
                    A(mqk[:, 4 * u:4 * u + 4, :], mqk[:, 4 * u:4 * u + 4, :], ACT.Silu).then_inc(mqk_ready, 1)
                for i in range(2):
                    await_drained(l, "lo", i)
                A(lo, lo, ACT.Sigmoid).then_inc(gate_ready, 1)
                ahead(l, "g0")
                sigmoid_gates(l, "g0")
                for t in range(NT):
                    b = await_full(l, "go", t)
                    A(tmp[:, t * W:(t + 1) * W], ps[:, b, :], ACT.Square).then_inc(gstat, 1)
                act.wait_ge(gstatv, l + 1)
                link(A(gn0, gvar, ACT.Ln))
                A(gy0, gn0, ACT.Exp, scale=-0.5).then_inc(gstat, 1)
                ahead(l, "g0'")
                await_drained(l, "mb", 1)
                A(mE, mE, ACT.Exp, scale=-1.0).then_inc(mEr, 1)
                sigmoid_gates(l, "g0'")
                ahead(l, "up0")
                for i in range(2):
                    hi_of(l, "yT1", i, yT_hi, C_GN)
                ahead(l, "g1")
                sigmoid_gates(l, "g1")
                ahead(l, "g1'")
                sigmoid_gates(l, "g1'")
                ahead(l, "up1")
                for i in range(2):
                    hi_of(l, "yT2", i, yT_hi)
                ahead(l, "g2")
                sigmoid_gates(l, "g2")
                ahead(l, "g2'")
                sigmoid_gates(l, "g2'")
                ahead(l, "up2")
                for i in range(4):
                    hi_of(l, "mgT", i, hT_hi)
                ahead(l, "wo")
                ahead(l, "wo'")
                for name in ("wo", "wo'"):
                    for t in range(NT):
                        await_drained(l, name, t)
                norm_stats()
                for i in range(4):
                    hi_of(l, "fnorm", i, hT_hi, C_FG)
                if l == 0:
                    for n, (kind, i, c) in enumerate(FF):
                        split_to(2 * NU + n + 2)
                        if kind == "gu" and c == 1:
                            for t in range(NT):
                                b = await_full(0, f"gu{i}", t)
                                A(silu_g[:, t, :], ps[:, b, 0:256], ACT.Silu).then_inc(silu_ready, 1)
                        if kind == "dn" and i + 1 < NF or kind == "gu" and c == 1 and i == 0:
                            i = i + 1 if kind == "dn" else 0
                            b = await_full(0, f"hT{i}")
                            copy(yT_hi[:, 2 * (i % 2):2 * (i % 2) + 2, :],
                                 ps[:, b, :].rearrange("p (m n) -> p m n", m=2)).then_inc(hi_part, 1)

            act.wait_ge(ws_in, 32 * L + 16)
            copy(ws_hi[:, 0:KT * E], ws_raw[:, 0:KT * E]).then_inc(ws_hi_ready, 1)
            act.wait_ge(router_d2, 1)
            A(g12[:, :, 0:1], g12[:, :, 0:1], ACT.Exp).then_inc(router_e, 1)

            def gather_hi(banks, waits):
                for i in range(2):
                    act.wait_ge(full[banks[i]], waits[i])
                    copy(hT_hi[:, 4 * i:4 * i + 4, 0:P], ps[:, banks[i], :].rearrange("p (m n) -> p m n", m=4))\
                        .then_inc(hi_part, 1)

            def moe_pass(pas):
                base = PASS_FILL[pas]
                gather_hi((6, 7), (base[6] + 1, base[7] + 1))
                with act.Fori(0, E) as e:
                    nsp = [0]

                    def split(n):
                        while nsp[0] <= min(n, FFC - 1):
                            j = nsp[0]
                            act.wait_ge(moe_in[j % RE],
                                        e * (32 * FFC // RE) + 32 * (pas * E * FFC // RE + j // RE + 1))
                            act.wait_ge(*moe_last_use(pas, e, j - RS))
                            copy(w_hi[:, j % RS, :], slot_raw(j, True)).then_inc(hi_ready, 1)
                            nsp[0] += 1

                    def moe_full(tag, i=0):
                        b, k = moe_fill(pas, e, tag, i)
                        act.wait_ge(full[b], k + 1)
                        return b

                    for n, (kind, i, c) in enumerate(FF):
                        split(n + 2)
                        if n == FFC - 1:
                            fb = [moe_fill(pas, e, "gather", q) for q in range(2)]
                            gather_hi([f[0] for f in fb], [f[1] + 1 for f in fb])
                            b = moe_full("acc", 0)
                            copy(ysb[:, 0:W], ps[:, b, :]).then_inc(drained[b], 1)
                        if kind == "gu" and c == 1:
                            b = moe_full(f"gu{i}")
                            A(silu_g[:, i % 2, :], ps[:, b, 0:256], ACT.Silu).then_inc(silu_ready, 1)
                        if kind == "dn" and i + 1 < NF or kind == "gu" and c == 1 and i == 0:
                            i = i + 1 if kind == "dn" else 0
                            b = moe_full(f"hT{i}")
                            copy(yT_hi[:, 2 * (i % 2):2 * (i % 2) + 2, 0:P],
                                 ps[:, b, 0:2 * P].rearrange("p (m n) -> p m n", m=2)).then_inc(hi_part, 1)
                for q in (6, 7):
                    act.wait_ge(drained[q], base[q] + PRO[q] + E * nexp[q] + EPI[q])

            moe_pass(0)
            many = act.value_load(cnt_i[0:1, 0:1], min_val=0, max_val=T)
            with act.If(many > P):
                moe_pass(1)
            norm_stats()

        @block.vector
        def _(dve):
            V = nc.vector
            tt, ts, stt = V.tensor_tensor, V.tensor_scalar, V.scalar_tensor_tensor
            seq, nsplit, nhi, nb, nnorm, nsilu = [0], [0], [0], [0], [0], [0]

            def note(ins):
                seq[0] += 1
                ins.then_inc(dve_seq, 1)

            def settle():
                dve.wait_ge(dve_seq, seq[0])

            def link(ins):
                note(ins)
                settle()

            def await_full(l, tag, i=0):
                b, k = FILL[l, tag, i]
                dve.wait_ge(full[b], k + 1)
                return b

            def await_drained(l, tag, i=0):
                b, k = FILL[l, tag, i]
                dve.wait_ge(drained[b], k + 1)

            def split_to(n):
                while nsplit[0] <= min(n, MOE_BASE - 1):
                    g = nsplit[0]
                    dve.wait_ge(hi_ready, g + 1)
                    tt(w_lo[:, g % RS, :], slot_raw(g, False), w_hi[:, g % RS, :], ALU.subtract)\
                        .then_inc(lo_ready, 1)
                    nsplit[0] += 1

            def ahead(l, name):
                split_to(LAYER_BASE[l] + 2 * UIDX[name] + 1 + 2)

            def rsqrt(y, v, t0, r):
                link(tt(t0, y, y, ALU.mult))
                link(tt(t0, t0, v, ALU.mult))
                link(ts(t0, t0, -0.5, 1.5, ALU.mult, ALU.add))
                link(tt(r, y, t0, ALU.mult))

            def norm_rows(gain=None):
                q = nnorm[0]
                nnorm[0] += 1
                dve.wait_ge(stat, 3 * q + 2)
                ts(var, ss, 1.0 / D, EPS, ALU.mult, ALU.add).then_inc(statv, 1)
                dve.wait_ge(stat, 3 * q + 3)
                rsqrt(y0, var, nt0, rstd)
                for t in range(NT):
                    if gain is None:
                        ts(xn[:, t, :], xt[:, t, :], rstd[:, t:t + 1], None, ALU.mult).then_inc(xn_ready, 1)
                    else:
                        stt(xn[:, t, :], xt[:, t, :], rstd[:, t:t + 1], gain, ALU.mult, ALU.mult)\
                            .then_inc(xn_ready, 1)

            def lo_of(l, tag, i, dst_hi, dst_lo, gain=None):
                b = await_full(l, tag, i)
                nhi[0] += 1
                dve.wait_ge(hi_part, nhi[0])
                if gain is None:
                    ins = tt(dst_lo[:, 2 * i:2 * i + 2, :], ps[:, b, :].rearrange("p (m n) -> p m n", m=2),
                             dst_hi[:, 2 * i:2 * i + 2, :], ALU.subtract)
                else:
                    for m in range(2):
                        k = 2 * i + m
                        ins = stt(dst_lo[:, k, :], ps[:, b, m * T:(m + 1) * T], cols[:, l, gain + k:gain + k + 1],
                                  dst_hi[:, k, :], ALU.mult, ALU.subtract)
                ins.then_inc(drained[b], 1)

            def biased(l, name, dst):
                s = nb[0] % 3
                dve.wait_ge(bias_in[s], 16 * (nb[0] // 3 + 1))
                nb[0] += 1
                for t in range(NT):
                    b = await_full(l, name, t)
                    tt(dst(t), ps[:, b, :], bias[:, s, :], ALU.add).then_inc(drained[b], 1)

            def merge(l, br):
                dve.wait_ge(gate_ready, NG * l + GATES[f"g{br}'"])
                for t in range(NT):
                    for h in range(2):
                        b = await_full(l, f"up{br}", 2 * t + h)
                        dst = gates[:, h, t, :] if br else xn[:, t, h * W:(h + 1) * W]
                        tt(dst, ps[:, b, :], gates[:, h, t, :], ALU.mult).then_inc(drained[b], 1)
                if br:
                    for t in range(NT):
                        for h in range(2):
                            await_drained(l, f"up{br}", 2 * t + h)
                            m = xn[:, t, h * W:(h + 1) * W]
                            ins = tt(m, m, gates[:, h, t, :], ALU.add)
                            if br == 2 and h == 1:
                                ins.then_inc(merged_ready, 1)
                            else:
                                note(ins)
                    settle()

            def soft_scores(l, g):
                for hh in range(4):
                    b = await_full(l, f"s{g}", hh)
                    tt(sc[:, g, hh, :], ps[:, b, 0:384], cmask[:, :], ALU.add).then_inc(drained[b], 1)
                for hh in range(4):
                    await_drained(l, f"s{g}", hh)
                note(V.reduce_max(mx[:, g, 1, :], sc[:, g, :, 0:T], AX))
                link(V.reduce_max(mx[:, g, 0, :], sc[:, g, :, T:T + P], AX))
                note(tt(sc[:, g, :, 0:T], sc[:, g, :, 0:T], mx[:, g, 1, :].unsqueeze(2).to_broadcast([P, 4, T]),
                        ALU.subtract))
                tt(sc[:, g, :, T:T + P], sc[:, g, :, T:T + P], mx[:, g, 0, :].unsqueeze(2).to_broadcast([P, 4, P]),
                   ALU.subtract).then_inc(sub_ready, 1)

            def row_sums(l, g):
                dve.wait_ge(p_ready, 2 * l + g + 1)
                note(V.reduce_sum(sums[:, g, 1, :], sc[:, g, :, 0:T], AX))
                link(V.reduce_sum(sums[:, g, 0, :], sc[:, g, :, T:T + P], AX))
                note(V.reciprocal(sums[:, g, :, :], sums[:, g, :, :]))

            def probs_out(l, g):
                for hh in (1, 3):
                    b = await_full(l, f"pT{g}", hh)
                    V.tensor_copy(pT[:, hh, :], ps[:, b, 0:384]).then_inc(drained[b], 1)

            def moba_rows(l, g):
                settle()
                for t in range(NT):
                    b = await_full(l, f"pv{g}", t)
                    tt(ytok[:, t, g * T:(g + 1) * T].rearrange("p (h n) -> p h n", h=4),
                       ps[:, b, 0:T].rearrange("p (h n) -> p h n", h=4),
                       sums[:, g, t, :].unsqueeze(2).to_broadcast([P, 4, HD]), ALU.mult).then_inc(drained[b], 1)

            def conv_taps(l, u):
                dve.wait_ge(conv0, 2 * l + u + 1)
                for i in range(1, 4):
                    for m in range(4 * u, 4 * u + 4):
                        c = C_CW + 4 * m + i
                        ins = stt(mqk[:, m, :], conv_in[:, m, i:i + T], cols[:, l, c:c + 1], mqk[:, m, :],
                                  ALU.mult, ALU.add)
                        if i < 3:
                            note(ins)
                        elif m % 4 == 3:
                            ins.then_inc(conv3, 1)
                        else:
                            note(ins)
                    settle()

            def small_parts(n, width):
                dve.wait_ge(ws_hi_ready, n)
                tt(ws_lo[:, 0:width], ws_raw[:, 0:width], ws_hi[:, 0:width], ALU.subtract).then_inc(ws_ready, 1)

            dve.wait_ge(c_in, 16)
            dve.wait_ge(c2_in, 32)
            dve.wait_ge(consts, 4)
            for l in range(L):
                split_to(LAYER_BASE[l] + RS - 1)
                norm_rows()
                small_parts(l + 1, KT * 24)
                for i in range(4):
                    lo_of(l, "norm", i, hT_hi, hT_lo, C_AG)
                ahead(l, "mq")
                biased(l, "mq", lambda t: zqk[:, t, 0:MIX])
                ahead(l, "mk")
                biased(l, "mk", lambda t: zqk[:, t, MIX:2 * MIX])
                b = await_full(l, "small")
                tt(zs[:, :, :], ps[:, b, 0:48].rearrange("p (t n) -> p t n", t=NT),
                   bsm[:, l, :].unsqueeze(1).to_broadcast([P, NT, 24]), ALU.add).then_inc(drained[b], 1)
                for t in range(NT):
                    await_drained(l, "mk", t)
                    await_drained(l, "mq", t)
                zh = zqk.rearrange("p t (h d) -> p t h d", d=HD)
                x1, x2 = zh[:, :, :, 0:8], zh[:, :, :, 8:16]
                cos, sin = (rope[:, i, :, :].unsqueeze(2).to_broadcast([P, NT, 16, 8]) for i in range(2))
                note(tt(rt[:, 0], x1, cos, ALU.mult))
                note(tt(rt[:, 1], x2, sin, ALU.mult))
                note(tt(rt[:, 2], x2, cos, ALU.mult))
                link(tt(rt[:, 3], x1, sin, ALU.mult))
                note(tt(x1, rt[:, 0], rt[:, 1], ALU.subtract))
                tt(x2, rt[:, 2], rt[:, 3], ALU.add).then_inc(rope_done, 1)
                ahead(l, "mv")
                biased(l, "mv", lambda t: vm[:, t, :])
                b = await_full(l, "smallT", 0)
                note(V.tensor_copy(aT[0:16, :], ps[0:16, b, 0:T]))
                V.tensor_copy(iT[0:4, :], ps[0:4, b, T:2 * T]).then_inc(drained[b], 1)
                b = await_full(l, "smallT", 1)
                V.tensor_copy(fT[0:4, :], ps[0:4, b, 0:T]).then_inc(drained[b], 1)
                for i in (2, 3):
                    b = await_full(l, "qkT", i)
                    V.tensor_copy(qkT[:, 2 * i:2 * i + 2, :], ps[:, b, :].rearrange("p (m n) -> p m n", m=2))\
                        .then_inc(drained[b], 1)
                ahead(l, "gqk")
                for i in range(2):
                    b = await_full(l, "gqk", i)
                    for m in (2 * i, 2 * i + 1):
                        ins = ts(gqk[:, m, :], ps[:, b, (m % 2) * T:(m % 2 + 1) * T],
                                 cols[:, l, C_BG + m:C_BG + m + 1], GD ** -0.5 if i == 0 else 1.0, ALU.add, ALU.mult)
                    ins.then_inc(drained[b], 1)
                ahead(l, "gv")
                biased(l, "gv", lambda t: vg[:, t, :])
                soft_scores(l, 0)
                ahead(l, "gr")
                biased(l, "gr", lambda t: gr[:, t, :])
                soft_scores(l, 1)
                row_sums(l, 0)
                ahead(l, "lq")
                probs_out(l, 0)
                moba_rows(l, 0)
                conv_taps(l, 0)
                ahead(l, "lk")
                row_sums(l, 1)
                probs_out(l, 1)
                moba_rows(l, 1)
                b = await_full(l, "ga")
                for m in range(2):
                    ins = ts(gA[:, m * T:(m + 1) * T], ps[:, b, m * T:(m + 1) * T],
                             cols[:, l, C_GB + m:C_GB + m + 1], None, ALU.add)
                ins.then_inc(drained[b], 1)
                conv_taps(l, 1)
                dve.wait_ge(lsg2, l + 1)
                note(stt(cumf[0:4, :], fT[0:4, :], 0.0, cumf[0:4, :], ALU.min, ALU.subtract))
                link(stt(gA, gA, 0.0, gB, ALU.min, ALU.subtract))
                note(V.tensor_tensor_scan(gC, chunk_start[:, :], gA, 0.0, ALU.mult, ALU.add))
                link(V.tensor_tensor_scan(fls[0:4, :], ones_row[0:4, :], cumf[0:4, :], 0.0, ALU.mult, ALU.add))
                note(tt(gl[0:4, :], iT[0:4, :], fls[0:4, :], ALU.subtract))
                gc = gC.rearrange("p (c n) -> p c n", n=CH)
                ce = gE.rearrange("p (c n) -> p c n", n=CH)
                tt(ce, gc[:, :, CH - 1:CH].to_broadcast([P, 2 * T // CH, CH]), gc, ALU.subtract).then_inc(gla_cum, 1)
                settle()
                link(V.tensor_tensor_scan(rmax[0:4, :], gl[0:4, :], gl[0:4, :], 0.0, ALU.max, ALU.max))
                tt(fls[0:4, :], fls[0:4, :], rmax[0:4, :], ALU.add).then_inc(rows_ready, 1)
                ahead(l, "lv")
                dve.wait_ge(gla_exp, l + 1)
                qd = gqk[:, 0:2, :]
                kk = gqk[:, 2:4, :]
                a3, b3, e3 = (v.rearrange("p (m n) -> p m n", m=2) for v in (gA, gB, gE))
                note(tt(b3, kk, b3, ALU.mult))
                note(tt(e3, kk, e3, ALU.mult))
                link(tt(qd, qd, a3, ALU.mult))
                for m in range(2):
                    e1, e2 = a3[:, m, 2 * CH - 1:2 * CH], a3[:, m, 3 * CH - 1:3 * CH]
                    note(ts(gx[:, m, 0:CH], qd[:, m, 2 * CH:3 * CH], e1, None, ALU.mult))
                    note(ts(gx[:, m, 2 * CH:3 * CH], qd[:, m, 3 * CH:4 * CH], e2, None, ALU.mult))
                settle()
                for m in range(2):
                    ins = ts(gx[:, m, CH:2 * CH], gx[:, m, 2 * CH:3 * CH], a3[:, m, 2 * CH - 1:2 * CH], None, ALU.mult)
                    if m:
                        ins.then_inc(gla_ops, 1)
                    else:
                        note(ins)
                biased(l, "lv", lambda t: vl[:, t, :])
                for i in range(2):
                    lo_of(l, "yT0", i, yT_hi, yT_lo)
                ahead(l, "lo")
                biased(l, "lo", lambda t: lo[:, t, :])
                dve.wait_ge(pads, 2 * l + 2)
                for h in range(4):
                    b = await_full(l, "gs", h)
                    V.copy_predicated(g_att[:, h, :], gmask[:, :], ps[:, b, 0:384]).then_inc(drained[b], 1)
                ahead(l, "g0")
                biased(l, "g0", lambda t: gates[:, 0, t, :])
                dve.wait_ge(gstat, 3 * l + 2)
                link(V.reduce_sum(gss, tmp[:, 0:2 * W].rearrange("p (h n) -> p h n", h=8), AX))
                ts(gvar, gss, 1.0 / 128, EPS, ALU.mult, ALU.add).then_inc(gstatv, 1)
                dve.wait_ge(gstat, 3 * l + 3)
                rsqrt(gy0, gvar, gn0, grs)
                for t in range(NT):
                    b = await_full(l, "go", t)
                    tt(ytok[:, t, :].rearrange("p (h n) -> p h n", h=4), ps[:, b, :].rearrange("p (h n) -> p h n", h=4),
                       grs[:, 4 * t:4 * t + 4].unsqueeze(2).to_broadcast([P, 4, P]), ALU.mult).then_inc(drained[b], 1)
                dve.wait_ge(gate_ready, NG * l + GATES["gr"])
                for t in range(NT):
                    await_drained(l, "go", t)
                    tt(ytok[:, t, :], ytok[:, t, :], gr[:, t, :], ALU.mult).then_inc(y_ready, 1)
                ahead(l, "g0'")
                biased(l, "g0'", lambda t: gates[:, 1, t, :])
                b2 = await_full(l, "mb", 2)
                V.tensor_copy(lcol, ps[:, b2, 0:16]).then_inc(drained[b2], 1)
                await_drained(l, "mb", 2)
                for i in range(2):
                    b = await_full(l, "mb", i)
                    for hh in range(2):
                        h = 2 * i + hh
                        ts(mE[:, h, 0:T], ps[:, b, hh * T:(hh + 1) * T], lcol[:, h:h + 1], 0.0, ALU.subtract, ALU.max)
                        ins = ts(mE[:, h, T:T + P], ps[:, b, hh * T + P:(hh + 1) * T], lcol[:, 4 + h:5 + h], 0.0,
                                 ALU.subtract, ALU.max)
                    ins.then_inc(drained[b], 1)
                ahead(l, "up0")
                dve.wait_ge(mEr, l + 1)
                note(tt(mE, mE, mmask[:, :].unsqueeze(1).to_broadcast([P, 4, 384]), ALU.mult))
                merge(l, 0)
                for i in range(2):
                    lo_of(l, "yT1", i, yT_hi, yT_lo, C_GN)
                settle()
                for h in range(4):
                    b = await_full(l, "ms", h)
                    stt(mW[:, h, :], ps[:, b, 0:384], MD ** -0.5, mE[:, h, :], ALU.mult, ALU.mult)\
                        .then_inc(drained[b], 1)
                ahead(l, "g1")
                biased(l, "g1", lambda t: gates[:, 0, t, :])
                ahead(l, "g1'")
                biased(l, "g1'", lambda t: gates[:, 1, t, :])
                b = await_full(l, "mo", 2)
                link(stt(lden, ps[:, b, 0:8], -1.0, lcol[:, 8:16], ALU.mult, ALU.max))
                tt(lden, ps[:, b, 0:8], lden, ALU.max).then_inc(drained[b], 1)
                await_drained(l, "mo", 2)
                link(V.reciprocal(lrin, lden))
                for t in range(NT):
                    b = await_full(l, "mo", t)
                    tt(ytok[:, t, :].rearrange("p (h n) -> p h n", h=4), ps[:, b, :].rearrange("p (h n) -> p h n", h=4),
                       lrin[:, 4 * t:4 * t + 4].unsqueeze(2).to_broadcast([P, 4, P]), ALU.mult).then_inc(drained[b], 1)
                dve.wait_ge(gate_ready, NG * l + GATES["lo"])
                for t in range(NT):
                    await_drained(l, "mo", t)
                    tt(ytok[:, t, :], ytok[:, t, :], lo[:, t, :], ALU.mult).then_inc(y_ready, 1)
                ahead(l, "up1")
                merge(l, 1)
                for i in range(2):
                    lo_of(l, "yT2", i, yT_hi, yT_lo)
                ahead(l, "g2")
                biased(l, "g2", lambda t: gates[:, 0, t, :])
                ahead(l, "g2'")
                biased(l, "g2'", lambda t: gates[:, 1, t, :])
                ahead(l, "up2")
                settle()
                merge(l, 2)
                for i in range(4):
                    lo_of(l, "mgT", i, hT_hi, hT_lo)
                for h, name in enumerate(("wo", "wo'")):
                    ahead(l, name)
                    for t in range(NT):
                        b = await_full(l, name, t)
                        r = xt[:, t, h * W:(h + 1) * W]
                        tt(r, r, ps[:, b, :], ALU.add).then_inc(drained[b], 1)
                for name in ("wo", "wo'"):
                    for t in range(NT):
                        await_drained(l, name, t)
                norm_rows()
                for i in range(4):
                    lo_of(l, "fnorm", i, hT_hi, hT_lo, C_FG)
                if l == 0:
                    for n, (kind, i, c) in enumerate(FF):
                        split_to(2 * NU + n + 2)
                        if kind == "gu" and c == 1:
                            for t in range(NT):
                                b = await_full(0, f"gu{i}", t)
                                nsilu[0] += 1
                                dve.wait_ge(silu_ready, nsilu[0])
                                tt(hid[:, t, :], silu_g[:, t, :], ps[:, b, 256:512], ALU.mult)\
                                    .then_inc(drained[b], 1)
                        if kind == "dn" and i + 1 < NF or kind == "gu" and c == 1 and i == 0:
                            i = i + 1 if kind == "dn" else 0
                            b = await_full(0, f"hT{i}")
                            nhi[0] += 1
                            dve.wait_ge(hi_part, nhi[0])
                            r = slice(2 * (i % 2), 2 * (i % 2) + 2)
                            tt(yT_lo[:, r, :], ps[:, b, :].rearrange("p (m n) -> p m n", m=2), yT_hi[:, r, :],
                               ALU.subtract).then_inc(drained[b], 1)
                    for t in range(NT):
                        for h in range(2):
                            b = await_full(0, "acc", 2 * t + h)
                            r = xt[:, t, h * W:(h + 1) * W]
                            tt(r, r, ps[:, b, :], ALU.add).then_inc(drained[b], 1)
                    for i in range(4):
                        await_drained(0, "acc", i)

            small_parts(L + 1, KT * E)
            dve.wait_ge(moe_consts, 2)
            dve.wait_ge(fg_in, 48)
            note(V.tensor_copy(iota, iota_i))
            for t in range(NT):
                note(tt(xn[:, t, :], xn[:, t, :], ffn_g, ALU.mult))
            b = await_full(1, "logits")
            tt(lg, ps[:, b, 0:NT * E].rearrange("p (t n) -> p t n", t=NT),
               rbias.unsqueeze(1).to_broadcast([P, NT, E]), ALU.add).then_inc(drained[b], 1)
            await_drained(1, "logits")
            for t in range(NT):
                note(V.max(m8[:, t, :], lg[:, t, :]))
            settle()
            tt(g12[:, :, 0:1], m8[:, :, 1:2], m8[:, :, 0:1], ALU.subtract).then_inc(router_d2, 1)
            for t in range(NT):
                note(V.max_index(idx[:, t, :], m8[:, t, :], lg[:, t, :]))
            settle()
            link(V.tensor_copy(idf, idx))
            dve.wait_ge(router_e, 1)
            link(ts(g12[:, :, 3:4], g12[:, :, 0:1], 1.0, None, ALU.add))
            link(V.reciprocal(g12[:, :, 1:2], g12[:, :, 3:4]))
            link(tt(g12[:, :, 2:3], g12[:, :, 0:1], g12[:, :, 1:2], ALU.mult))
            for t in range(NT):
                for a in range(2):
                    note(ts(oh[:, a, t, :], iota[:, 0:E], idf[:, t, a:a + 1], None, ALU.is_equal))
            settle()
            tt(ind, oh[:, 0, :, :], oh[:, 1, :, :], ALU.add).then_inc(ind_ready, 1)
            dve.wait_ge(ind_ready, 1)
            for t in range(NT):
                for a in range(2):
                    note(ts(oh[:, a, t, :], oh[:, a, t, :], g12[:, t, 1 + a:2 + a], None, ALU.mult))
            settle()
            for s in range(2):
                note(tt(gmat[:, :, s * E:(s + 1) * E], oh[:, 0, :, :], oh[:, 1, :, :], ALU.add))
            b = await_full(1, "rank")
            note(stt(pos[:, :, 0:E], ps[:, b, 0:NT * E].rearrange("p (t n) -> p t n", t=NT), 1.0, ind, ALU.add, ALU.mult))
            V.reduce_max(g12[:, 0, 0:1], ps[:, b, 2 * E:3 * E], AX).then_inc(drained[b], 1)
            await_drained(1, "rank")
            settle()
            note(ts(pos[:, :, E:2 * E], pos[:, :, 0:E], -1.0 - P, None, ALU.add))
            link(ts(pos[:, :, 0:E], pos[:, :, 0:E], -1.0, None, ALU.add))
            V.tensor_copy(cnt_i[:, :], g12[:, 0, 0:1]).then_inc(pos_ready, 1)

            def select(col, done):
                for t in range(NT):
                    pc, gc = pos[:, t, col], gmat[:, t, col]
                    ts(selg[:, t, :], iota, pc, gc, ALU.is_equal, ALU.mult)
                    ins = ts(sel[:, t, :], iota, pc, None, ALU.is_equal)
                ins.then_inc(sel_ready, 1)

            def gather_lo(banks, waits, nh):
                for i in range(2):
                    dve.wait_ge(full[banks[i]], waits[i])
                    dve.wait_ge(hi_part, nh + i + 1)
                    r = slice(4 * i, 4 * i + 4)
                    tt(hT_lo[:, r, 0:P], ps[:, banks[i], :].rearrange("p (m n) -> p m n", m=4), hT_hi[:, r, 0:P],
                       ALU.subtract).then_inc(drained[banks[i]], 1)

            HI0 = nhi[0]
            HIX = NF + 2

            def moe_pass(pas):
                base = PASS_FILL[pas]
                hb = HI0 + pas * (2 + E * HIX)
                V.memset(selT, 0.0)
                V.memset(ysb, 0.0).then_inc(zeroed, 1)
                select(slice(pas * E, pas * E + 1), None)
                gather_lo((6, 7), (base[6] + 1, base[7] + 1), hb)

                def add_rows(fill):
                    for t in range(NT):
                        for h in range(2):
                            b, k = fill(t, h)
                            dve.wait_ge(full[b], k + 1)
                            dve.wait_ge(drained[b], k)
                            r = xt[:, t, h * W:(h + 1) * W]
                            tt(r, r, ps[:, b, :], ALU.add).then_inc(drained[b], 1)

                with dve.Fori(0, E) as e:
                    nsp, nh = [0], [0]

                    def split(n):
                        while nsp[0] <= min(n, FFC - 1):
                            j = nsp[0]
                            dve.wait_ge(hi_ready, e * FFC + (MOE_BASE + pas * E * FFC + j + 1))
                            tt(w_lo[:, j % RS, :], slot_raw(j, True), w_hi[:, j % RS, :], ALU.subtract)\
                                .then_inc(lo_ready, 1)
                            nsp[0] += 1

                    def moe_full(tag, i=0):
                        b, k = moe_fill(pas, e, tag, i)
                        dve.wait_ge(full[b], k + 1)
                        return b

                    for n, (kind, i, c) in enumerate(FF):
                        split(n + 2)
                        if n == FFC - 1:
                            fb = [moe_fill(pas, e, "gather", q) for q in range(2)]
                            gather_lo([f[0] for f in fb], [f[1] + 1 for f in fb], e * HIX + (hb + 2 + nh[0]))
                            nh[0] += 2
                            b = moe_full("acc", 1)
                            V.tensor_copy(ysb[:, W:2 * W], ps[:, b, :]).then_inc(drained[b], 1)
                        if kind == "gu" and c == 1:
                            b = moe_full(f"gu{i}")
                            dve.wait_ge(silu_ready, e * NF + (NT * NF + pas * E * NF + i + 1))
                            tt(hid[:, i % 2, :], silu_g[:, i % 2, :], ps[:, b, 256:512], ALU.mult)\
                                .then_inc(drained[b], 1)
                            if i == 0:
                                add_rows(lambda t, h: moe_fill(pas, e, f"sc{t}", h))
                        if kind == "dn" and i + 1 < NF or kind == "gu" and c == 1 and i == 0:
                            ih = i + 1 if kind == "dn" else 0
                            b = moe_full(f"hT{ih}")
                            dve.wait_ge(hi_part, e * HIX + (hb + 2 + nh[0] + 1))
                            nh[0] += 1
                            r = slice(2 * (ih % 2), 2 * (ih % 2) + 2)
                            tt(yT_lo[:, r, 0:P], ps[:, b, 0:2 * P].rearrange("p (m n) -> p m n", m=2),
                               yT_hi[:, r, 0:P], ALU.subtract).then_inc(drained[b], 1)
                        if kind == "dn" and i == 4:
                            b = moe_full("selT")
                            V.tensor_copy(selT, ps[:, b, 0:2 * P]).then_inc(drained[b], 1)
                            select(bass.ds(e + (pas * E + 1), 1), None)
                    assert nh[0] == HIX
                add_rows(lambda t, h: (6 + h, base[6 + h] + PRO[6] + E * nexp[6 + h] + t))
                for q in (6, 7):
                    dve.wait_ge(drained[q], base[q] + PRO[q] + E * nexp[q] + EPI[q])

            moe_pass(0)
            many = dve.value_load(cnt_i[0:1, 0:1], min_val=0, max_val=T)
            with dve.If(many > P):
                moe_pass(1)
            norm_rows(fin_g)


def kernel(**inputs):
    import concourse.bacc as bacc
    from concourse import mybir
    from concourse.bass_utils import run_bass_kernel_spmd

    L, D, _ = inputs["w_in"].shape
    T, P, KT = inputs["x"].shape[1], 128, D // 128
    a = {k: np.ascontiguousarray(v) for k, v in inputs.items()}

    def column(v, tiles):
        return v.reshape(L, tiles, P).transpose(0, 2, 1)

    b = a["b_in"]
    conv_w = a["mlstm_conv_w"].transpose(0, 2, 1).reshape(L, 8, P, 4).transpose(0, 2, 1, 3).reshape(L, P, 32)
    cols = np.concatenate([column(a["attn_norm_g"], KT), column(a["ffn_norm_g"], KT), conv_w,
                           column(a["mlstm_conv_b"], 8), column(b[:, 1536:2048], 4), column(b[:, 3088:4112], 8),
                           column(a["gla_gate_b"], 2), column(a["gla_norm_g"], 4)], axis=2)
    small = [slice(2560, 2576), slice(4624, 4632)]
    w_small = np.concatenate([a["w_in"][:, :, s] for s in small], axis=2)
    w_small = w_small.reshape(L, KT, P, 24).transpose(0, 2, 1, 3).reshape(L, P, KT * 24)
    b_small = np.concatenate([b[:, s] for s in small], axis=1)
    router = a["router_w"][0].reshape(KT, P, -1).transpose(1, 0, 2).reshape(P, -1)
    inv = np.power(np.float32(500000.0), -np.arange(8, dtype=np.float32) * np.float32(2.0) / np.float32(16))
    ang = np.arange(T, dtype=np.float32)[:, None] * inv[None, :].astype(np.float32)
    rope = np.stack([np.cos(ang), np.sin(ang)]).astype(np.float32)
    rope = rope.reshape(2, T // P, P, 8).transpose(2, 0, 1, 3)

    nc = bacc.Bacc("TRN2", target_bir_lowering=False, num_devices=1)
    arrays = {}

    def dram(name, v):
        v = np.ascontiguousarray(v)
        arrays[name + "_dram"] = v
        return nc.dram_tensor(name + "_dram", v.shape, mybir.dt.from_np(v.dtype), kind="ExternalInput").ap()

    args = [dram("x", a["x"][0]), dram("w_in", a["w_in"]), dram("b_in", b), dram("cols", cols),
            dram("w_small", w_small), dram("b_small", b_small), dram("gate_w", a["gla_gate_w"]),
            [dram(n, a[n]) for n in ("w_up_moba", "w_up_gla", "w_up_mlstm")], dram("w_o", a["w_o"]),
            dram("ffn_gate", a["ffn_w_gate"][0]), dram("ffn_up", a["ffn_w_up"][0]), dram("ffn_down", a["ffn_w_down"][0]),
            dram("router", router), dram("router_b", a["router_b"][0]), dram("moe_gate", a["moe_w_gate"][0]),
            dram("moe_up", a["moe_w_up"][0]), dram("moe_down", a["moe_w_down"][0]),
            dram("ffn_norm_g", a["ffn_norm_g"]), dram("final_g", a["final_norm_g"]), dram("rope", rope)]
    out = nc.dram_tensor("out_dram", (T, D), mybir.dt.float32, kind="ExternalOutput").ap()
    program(nc, *args, out)
    r = run_bass_kernel_spmd(nc, [arrays], core_ids=[0])
    return r.results[0]["out_dram"].reshape(1, T, D)
```

```python
import numpy as np


def program(nc, x, w_in, b_in, cols_d, w_small_d, gate_w, w_up, w_o, ffn_gate, ffn_up, ffn_down,
            router_d, router_b, moe_gate, moe_up, moe_down, ffn_norm_g, final_g, rope_d, out):
    import concourse.bass as bass
    from concourse import mybir
    from contextlib import ExitStack

    f32, f32r, bf16 = mybir.dt.float32, mybir.dt.float32r, mybir.dt.bfloat16
    i8, i32, u32 = mybir.dt.int8, mybir.dt.int32, mybir.dt.uint32
    ACT, ALU, AX = mybir.ActivationFunctionType, mybir.AluOpType, mybir.AxisListType.X

    P = 128
    T, D = x.shape
    NT = T // P
    L = w_in.shape[0]
    MIX = D // 2
    KT = D // P
    F = ffn_gate.shape[1]
    E = moe_gate.shape[0]
    HD = 64
    GD = 64
    CH = 64
    MD = 128
    EPS = 1e-6
    TAU = 16.0
    W = 512
    CK = 2048
    names = (("mq", MIX), ("mk", MIX), ("mv", MIX), ("gqk", MIX), ("gv", MIX), ("ga", 16), ("gr", MIX),
             ("lq", MIX), ("lk", MIX), ("lv", MIX), ("li", 4), ("lf", 4), ("lo", MIX), ("mg", 3 * D))
    OFF, at_col = {}, 0
    for name, size in names:
        OFF[name] = at_col
        at_col += size
    C_AG, C_FG, C_CW, C_CB, C_BG, C_BL, C_GB, C_GN, C_SB = 0, 8, 16, 48, 56, 60, 68, 70, 74
    SW = w_small_d.shape[2] // (D // 128)
    SMALL = ((0, 4), (32, 4), (64, 16))
    NCOL = cols_d.shape[2]

    UNITS = [("mq", OFF["mq"]), ("mk", OFF["mk"]), ("mv", OFF["mv"]), ("gqk", OFF["gqk"]), ("gv", OFF["gv"]),
             ("gr", OFF["gr"]), ("lq", OFF["lq"]), ("lk", OFF["lk"]), ("lv", OFF["lv"]), ("lo", OFF["lo"])]
    for b in range(3):
        UNITS += [(f"g{b}", OFF["mg"] + b * D), (f"g{b}'", OFF["mg"] + b * D + W), (f"up{b}", b)]
    UNITS += [("wo", 0), ("wo'", W)]
    UIDX = {name: i for i, (name, _) in enumerate(UNITS)}
    FEATURE_MAJOR = ("gqk", "lq", "lk")
    BIASED = [n for n, _ in UNITS if n[:2] not in ("up", "wo") and n not in FEATURE_MAJOR]
    NU = len(UNITS)
    NAMES = [n for n, _ in UNITS]
    ORDER = [(n, c) for n in NAMES[:NAMES.index("up2")] if n != "g2'" for c in range(2)]
    ORDER += [("g2'", 0), ("up2", 0), ("g2'", 1), ("up2", 1), ("wo", 0), ("wo'", 0), ("wo", 1), ("wo'", 1)]
    CPOS = {key: i for i, key in enumerate(ORDER)}
    assert len(ORDER) == 2 * NU
    NF = F // 256
    FFC = 3 * NF
    LAYER_BASE = [0, 2 * NU + FFC]
    MOE_BASE = LAYER_BASE[1] + 2 * NU
    RM, RE, RS = 3, 11, 3
    assert FFC % RE == 0 and FFC % RS == 0 and MOE_BASE % RS == 0 and L == 2 and F % 256 == 0

    FF = []
    for i in range(NF + 1):
        if i < NF:
            FF += [("gu", i, 0), ("gu", i, 1)]
        if i:
            FF += [("dn", i - 1, 0)]

    FILL, nfill = {}, [0] * 8

    def fills(l, tag, banks):
        for i, b in enumerate(banks):
            FILL[l, tag, i] = (b, nfill[b])
            nfill[b] += 1

    A4 = (4, 5, 6, 7)
    for l in range(L):
        for tag, banks in (
                ("norm", A4), ("mq", (0, 1)), ("rb", (5,)), ("mk", (2, 3)), ("small", (4,)), ("mv", (0, 1)),
                ("qkT", A4), ("gqk", (2, 3)), ("gv", (0, 1)), ("s0", A4), ("gr", (2, 3)), ("s1", A4),
                ("lq", (0, 1)), ("ga", (7,)), ("lk", (2, 3)), ("pT0", A4), ("lv", (0, 1)), ("pv0", (4, 5)),
                ("pT1", (6, 7, 4, 5)), ("lo", (2, 3)), ("pv1", (4, 5)), ("g0", (0, 1)), ("lc", (6,)),
                ("gs", (4, 5, 7, 6)), ("yT0", (4, 5)), ("g0'", (2, 3)), ("go", (4, 5)), ("mb", (6, 7)),
                ("up0", (0, 1, 2, 3)), ("yT1", (4, 5)), ("g1", (0, 1)), ("ms", (6, 7, 4, 5)), ("g1'", (2, 3)),
                ("up1", (0, 1, 2, 3)), ("mo", (4, 5, 6)), ("g2", (0, 1)), ("yT2", (4, 5)), ("up2", (6, 7, 0, 1)),
                ("g2'", (2, 3)), ("mgT", A4), ("wo", (2, 3)), ("wo'", (0, 1)), ("fnorm", A4)):
            fills(l, tag, banks)
        if l == 0:
            for i in range(NF):
                b = 2 * (1 - i % 2)
                fills(0, f"gu{i}", (b, b + 1))
                fills(0, f"hT{i}", (b,))
            fills(0, "acc", A4)
    fills(1, "logits", (0,))
    fills(1, "lgT", (1,))
    fills(1, "rank", (0,))
    EXPERT, nexp = {}, [0] * 8

    def efills(tag, banks):
        for i, b in enumerate(banks):
            EXPERT[tag, i] = (b, nexp[b])
            nexp[b] += 1

    for i in range(NF):
        efills(f"gu{i}", (i % 2,))
        efills(f"hT{i}", (2,))
    efills("selT", (3,))
    efills("acc", (4, 5))
    efills("sc0", (6, 7))
    efills("sc1", (6, 7))
    efills("gather", (6, 7))
    PRO, EPI = {6: 1, 7: 1}, {6: 2, 7: 2}
    PASS_FILL = [[nfill[b] for b in range(8)]]
    PASS_FILL.append([PASS_FILL[0][b] + E * nexp[b] + PRO.get(b, 0) + EPI.get(b, 0) for b in range(8)])

    USED, n_used = [], 0
    for l in range(L):
        for name, c in ORDER:
            if name[:2] == "up":
                USED.append(("bank", (l, name, 2 * c + 1)))
            elif c:
                USED.append(("bank", (l, name, 1)))
            else:
                n_used += 1
                USED.append(("w", n_used))
        if l == 0:
            for kind, i, c in FF:
                if kind == "gu" and c == 1:
                    USED.append(("bank", (0, f"gu{i}", 1)))
                elif kind == "dn" and i == NF - 1:
                    USED.append(("bank", (0, "acc", 3)))
                else:
                    n_used += 1
                    USED.append(("w", n_used))
    MOE_USED0 = n_used
    EUSED, eu = [], 0
    for kind, i, c in FF:
        if kind == "gu" and c == 1:
            EUSED.append(("bank", (f"gu{i}", 0)))
        elif kind == "dn" and i == NF - 1:
            EUSED.append(("bank", ("acc", 1)))
        else:
            eu += 1
            EUSED.append(("w", eu))
    EU = eu

    ctx = ExitStack()
    with ctx:
        def sb(name, shape, dt=f32):
            return ctx.enter_context(nc.sbuf_tensor(name, shape, dt))

        def sem(name):
            return ctx.enter_context(nc.semaphore(name))

        raw_m = sb("raw_m", [P, RM, CK])
        late = sb("late", [P, (RE - RM) * CK])
        w_hi = sb("w_hi", [P, RS, CK], f32r)
        w_lo = sb("w_lo", [P, RS, CK], f32r)
        xt = sb("xt", [P, NT, D])
        xn = sb("xn", [P, NT, D])
        hT_hi = sb("hT_hi", [P, KT, T], f32r)
        hT_lo = sb("hT_lo", [P, KT, T], f32r)
        yT_hi = sb("yT_hi", [P, 4, T], f32r)
        yT_lo = sb("yT_lo", [P, 4, T], f32r)
        ytok = sb("ytok", [P, NT, MIX])
        bias = sb("bias", [P, 3, W])
        tmp = sb("tmp", [P, 3072])
        ident = sb("ident", [P, P])
        cols = sb("cols", [P, L, NCOL])
        cmask = sb("cmask", [P, 384], bf16)
        mmask = sb("mmask", [P, 384], bf16)
        gmask = sb("gmask", [P, 384], i8)
        chunk_start = sb("chunk_start", [P, 2 * T], bf16)
        sel4 = sb("sel4", [4, 4, P], f32r)
        rmax_hi = sb("rmax_hi", [4, T], f32r)
        rmax_lo = sb("rmax_lo", [4, T], f32r)
        ones = sb("ones", [P, 2])
        gw = sb("gw", [16, T])
        st = sb("st", [P, 128])
        cnt_i = sb("cnt_i", [P, 1], i32)

        at = [0]

        def piece(n):
            at[0] += n
            assert at[0] <= late.shape[1]
            return late[:, at[0] - n:at[0]]

        zqk_flat = piece(8 * (T + 3))
        zqk = zqk_flat[:, 0:NT * 2 * MIX].rearrange("p (t n) -> p t n", t=NT)
        conv_in = zqk_flat.rearrange("p (m n) -> p m n", m=8)
        qkT_flat = piece(8 * T)
        qkT = qkT_flat.rearrange("p (m n) -> p m n", m=8)
        g_att = qkT_flat[:, 0:1536].rearrange("p (h n) -> p h n", h=4)
        sel4_f = qkT_flat[0:4, 0:4 * P].rearrange("p (h n) -> p h n", h=4)
        gz = qkT_flat[:, 1536:2048]
        vm = piece(NT * MIX).rearrange("p (t n) -> p t n", t=NT)
        vg = piece(NT * MIX).rearrange("p (t n) -> p t n", t=NT)
        vl = piece(NT * MIX).rearrange("p (t n) -> p t n", t=NT)
        gr = piece(NT * MIX).rearrange("p (t n) -> p t n", t=NT)
        lo = piece(NT * MIX).rearrange("p (t n) -> p t n", t=NT)
        gqk = piece(4 * T).rearrange("p (m n) -> p m n", m=4)
        mqk_flat = piece(8 * T)
        mqk = mqk_flat.rearrange("p (m n) -> p m n", m=8)
        gates_flat = piece(2 * NT * W)
        gates = gates_flat.rearrange("p (a t n) -> p a t n", a=2, t=NT)
        pT = gates_flat[:, 0:1536].rearrange("p (h n) -> p h n", h=4)
        rows = piece(7 * T).rearrange("p (m n) -> p m n", m=7)
        rope = piece(2 * NT * 8).rearrange("p (a t n) -> p a t n", a=2, t=NT)
        aT, iT, fT, cumf, gl, rmax, fls = (rows[:, i] for i in range(7))
        sc = tmp[:, :].rearrange("p (g h n) -> p g h n", g=2, h=4)
        rt = tmp[:, 0:1024].rearrange("p (m t h n) -> p m t h n", m=4, t=NT, h=16)
        gA, gB, gC, gE = (tmp[:, i * 512:(i + 1) * 512] for i in range(4))
        gx = tmp[:, 2048:2048 + 384].rearrange("p (m n) -> p m n", m=2)
        mE = tmp[:, 0:1536].rearrange("p (h n) -> p h n", h=4)
        mW = tmp[:, 1536:3072].rearrange("p (h n) -> p h n", h=4)
        ws_raw = tmp[:, 0:KT * SW]
        ws_hi = yT_hi[:, :, :].rearrange("p m n -> p (m n)")
        ws_lo = yT_lo[:, :, :].rearrange("p m n -> p (m n)")
        silu_g = ytok[:, 0, :].rearrange("p (t n) -> p t n", t=NT)
        hid = ytok[:, 1, :].rearrange("p (t n) -> p t n", t=NT)
        lgT = tmp[0:E, 512:512 + T]
        ysb_hi, ysb_lo = hT_hi[:, :, P:2 * P], hT_lo[:, :, P:2 * P]
        selT = yT_hi[:, 0:NT, P:2 * P]
        fin_g = tmp[:, D:2 * D]
        ffn_g = tmp[:, 2 * D:3 * D]
        bflat = bias[:, :, :].rearrange("p a n -> p (a n)")
        sel = bflat[:, 0:256].rearrange("p (t n) -> p t n", t=NT)
        zeros = bflat[:, 256:384]
        gcur = bflat[:, 512:514]
        gslot = bflat[:, 520:521]
        iota = bflat[:, 768:896]
        tri = bflat[:, 896:1024]
        allones = bflat[:, 1024:1152]
        iota_i = bflat[:, 1152:1280].bitcast(i32)
        pos = bflat[:, 1280:1280 + 34].rearrange("p (t n) -> p t n", t=NT)
        gmat = bflat[:, 1320:1320 + 34].rearrange("p (t n) -> p t n", t=NT)
        ind = bflat[:, 1360:1376].rearrange("p (t n) -> p t n", t=NT)
        lg = bflat[:, 1376:1392].rearrange("p (t n) -> p t n", t=NT)
        m8 = bflat[:, 1392:1408].rearrange("p (t n) -> p t n", t=NT)
        idx = bflat[:, 1408:1424].bitcast(u32).rearrange("p (t n) -> p t n", t=NT)
        idf = bflat[:, 1424:1440].rearrange("p (t n) -> p t n", t=NT)
        oh = bflat[:, 1440:1472].rearrange("p (a t n) -> p a t n", a=2, t=NT)
        rbias = bflat[:, 1480:1488]
        g12 = bflat[:, 1488:1496].rearrange("p (t n) -> p t n", t=NT)
        ss, var, y0, nt0 = (st[:, 2 * i:2 * i + 2] for i in range(4))
        idle = st[:, 14:16]
        ss1, var0 = st[:, 10:12], st[:, 12:14]
        rstds = st[:, 120:128].rearrange("p (q t) -> p q t", t=NT)
        rfin = st[:, 8:10]
        rb = ytok[:, 0, 0:T]
        rcol = ytok[:, 1, 0:T].rearrange("p (t n) -> p t n", t=NT)
        mx = st[:, 16:32].rearrange("p (g t h) -> p g t h", g=2, t=NT)
        sums = st[:, 32:48].rearrange("p (g t h) -> p g t h", g=2, t=NT)
        gss, gvar, gy0, gn0, grs = (st[:, 48 + 8 * i:56 + 8 * i] for i in range(5))
        lcol = st[:, 88:104]
        lden, lrin = st[:, 104:112], st[:, 112:120]

        def slot_raw(n, moe):
            s = n % (RE if moe else RM)
            return raw_m[:, s, :] if s < RM else late[:, (s - RM) * CK:(s - RM + 1) * CK]

        ps = ctx.enter_context(nc.psum_tensor("ps", [P, 8, W], f32))

        raw_in = [sem(f"raw_in{i}") for i in range(RM)]
        moe_in = [sem(f"moe_in{i}") for i in range(RE)]
        hi_ready = sem("w_hi_ready")
        lo_ready = sem("w_lo_ready")
        w_used = sem("w_used")
        full = [sem(f"bank_full{i}") for i in range(8)]
        drained = [sem(f"bank_drained{i}") for i in range(8)]
        bias_in = [sem(f"bias_in{i}") for i in range(3)]
        c_in = sem("columns_in")
        c2_in = sem("constants_in")
        x_in = [sem(f"x_half_in{i}") for i in range(2)]
        ws_in = sem("small_weights_in")
        fg_in = sem("norm_gains_in")
        consts = sem("masks_built")
        moe_consts = sem("moe_tables_built")
        pads = sem("conv_pads_zeroed")
        act_seq = sem("act_seq")
        dve_seq = sem("dve_seq")
        out_done = sem("out_done")
        final_rows = sem("final_rows")
        rfin_ready = sem("final_rstd")
        scaled = [sem(f"final_tile{i}_scaled") for i in range(NT)]
        stat = sem("row_stats_ready")
        statv = sem("row_stats_scaled")
        rstd_ready = sem("rstd_ready")
        rb_ready = sem("rstd_columns_ready")
        hi_part = sem("hi_part_ready")
        ws_hi_ready = sem("small_hi_ready")
        ws_ready = sem("small_ready")
        rope_done = sem("rope_done")
        p_ready = sem("probs_ready")
        y_ready = sem("y_gla_mlstm_ready")
        lsg2 = sem("log_sigmoid_done")
        gla_cum = sem("gla_cumsum")
        gla_exp = sem("gla_exps")
        gla_ops = sem("gla_operands")
        rows_ready = sem("mlstm_rows_ready")
        floors = sem("mlstm_floors")
        mEr = sem("mlstm_decays")
        conv0 = sem("conv_first_tap")
        conv3 = sem("conv_taps_done")
        mqk_ready = sem("mqk_ready")
        gate_ready = sem("gates_ready")
        sub_ready = sem("scores_shifted")
        gstat = sem("gla_stats_ready")
        gstatv = sem("gla_stats_scaled")
        GATES = {"gr": 1, "lo": 2}
        for b in range(3):
            GATES[f"g{b}"] = 4 + 4 * b
            GATES[f"g{b}'"] = 6 + 4 * b
        NG = 14
        merged_ready = sem("merged_ready")
        silu_ready = sem("silu_ready")
        router_e = sem("router_exp")
        router_d2 = sem("router_gap")
        ind_ready = sem("picks_ready")
        pos_ready = sem("positions_ready")
        sel_ready = sem("selection_ready")
        zeroed = sem("expert_rows_zeroed")

        block = ctx.enter_context(nc.Block())

        def last_use(n):
            kind, v = USED[n]
            if kind == "w":
                return w_used, v
            b, k = FILL[v]
            return full[b], k + 1

        def moe_last_use(pas, e, j):
            kind, v = EUSED[j % FFC]
            back = -1 if j < 0 else 0
            if kind == "w":
                return w_used, MOE_USED0 + (pas * E + back) * EU + v + e * EU
            b, k = EXPERT[v]
            return full[b], PASS_FILL[pas][b] + PRO.get(b, 0) + k + 1 + back * nexp[b] + e * nexp[b]

        def moe_fill(pas, e, tag, i):
            b, k = EXPERT[tag, i]
            return b, PASS_FILL[pas][b] + PRO.get(b, 0) + k + e * nexp[b]

        @block.sync
        def _(sp):
            def load_x(h):
                for t in range(NT):
                    sp.dma_start(xt[:, t, h * W:(h + 1) * W], x[t * P:(t + 1) * P, h * W:(h + 1) * W])\
                        .then_inc(x_in[h], 16)

            sp.dma_start(cols[:, :, :], cols_d.rearrange("l p n -> p l n")).then_inc(c_in, 16)
            load_x(0)

            def source(l, n):
                name, c = ORDER[n]
                o = UNITS[UIDX[name]][1]
                if name[:2] == "up":
                    return w_up[o][l, :, c * W:(c + 1) * W].rearrange("(k p) n -> p k n", p=P)
                m = w_o if name[:2] == "wo" else w_in
                return m[l, 4 * c * P:4 * (c + 1) * P, o:o + W].rearrange("(k p) n -> p k n", p=P)

            def load_ff(dst, g, u, d, kind, i, c, done):
                if kind == "gu":
                    v = dst.rearrange("p (k n) -> p k n", k=4)
                    for half, m in enumerate((g, u)):
                        sp.dma_start(v[:, :, half * 256:(half + 1) * 256],
                                     m(slice(4 * c * P, 4 * (c + 1) * P), slice(i * 256, (i + 1) * 256))
                                     .rearrange("(k p) n -> p k n", p=P)).then_inc(done, 16)
                else:
                    v = dst.rearrange("p (k n) -> p k n", k=2)
                    for k in range(2):
                        sp.dma_start(v[:, k, :], d(slice(i * 256 + k * P, i * 256 + (k + 1) * P), slice(0, D)))\
                            .then_inc(done, 16)

            for l in range(L):
                for n in range(2 * NU):
                    g = LAYER_BASE[l] + n
                    if g >= RM:
                        sp.wait_ge(lo_ready, g - RM + 1)
                    s = source(l, n)
                    k = s.shape[1]
                    v = slot_raw(g, False).rearrange("p (k n) -> p k n", k=k)
                    for h in range(2):
                        sp.dma_start(v[:, h * k // 2:(h + 1) * k // 2, :], s[:, h * k // 2:(h + 1) * k // 2, :])\
                            .then_inc(raw_in[g % RM], 16)
                    if g == 0:
                        load_x(1)
                if l == 0:
                    for n, (kind, i, c) in enumerate(FF):
                        g = 2 * NU + n
                        sp.wait_ge(lo_ready, g - RM + 1)
                        load_ff(slot_raw(g, False), lambda r, q: ffn_gate[r, q], lambda r, q: ffn_up[r, q],
                                lambda r, q: ffn_down[r, q], kind, i, c, raw_in[g % RM])
            sp.wait_ge(lo_ready, MOE_BASE)
            sp.wait_ge(merged_ready, L * NT)

            def moe_loads(pas):
                with sp.Fori(0, E) as e:
                    for j, (kind, i, c) in enumerate(FF):
                        sp.wait_ge(lo_ready, e * FFC + (MOE_BASE + pas * E * FFC + j - RE + 1))

                        def view(m):
                            return lambda r, q: m[bass.ds(e, 1), r, q].rearrange("a r q -> (a r) q")
                        load_ff(slot_raw(j, True), view(moe_gate), view(moe_up), view(moe_down), kind, i, c,
                                moe_in[j % RE])

            moe_loads(0)
            sp.wait_ge(pos_ready, 1)
            many = sp.value_load(cnt_i[0:1, 0:1], min_val=0, max_val=T)
            with sp.If(many > P):
                moe_loads(1)
            for h in range(2):
                for t in range(NT):
                    sp.wait_ge(scaled[t], h + 1)
                    sp.dma_start(out[t * P:(t + 1) * P, h * W:(h + 1) * W], xn[:, t, h * W:(h + 1) * W])\
                        .then_inc(out_done, 16)
            sp.wait_ge(out_done, 32 * NT)

        @block.gpsimd
        def _(pool):
            built = 0

            def fence(ins):
                nonlocal built
                ins.then_inc(consts, 1)
                built += 1
                pool.wait_ge(consts, built)

            fence(nc.gpsimd.memset(ident[:, :], 0.0))
            fence(nc.gpsimd.affine_select(out=ident[:, :], in_=ident[:, :], compare_op=ALU.not_equal, fill=1.0,
                                          base=0, pattern=[[-1, P]], channel_multiplier=1))
            pool.dma_start(ws_raw, w_small_d[0]).then_inc(ws_in, 16)
            pool.dma_start(gw[0:16, :], gate_w[0]).then_inc(ws_in, 16)
            pool.dma_start(bias[:, 0, :], b_in[0, OFF["mq"]:OFF["mq"] + W].partition_broadcast(P))\
                .then_inc(bias_in[0], 16)
            pool.dma_start(rope[:, :, :, :], rope_d).then_inc(c2_in, 16)
            nc.gpsimd.memset(ones[:, :], 1.0)
            nc.gpsimd.memset(cmask[:, :], 0.0)
            nc.gpsimd.memset(mmask[:, :], 1.0)
            nc.gpsimd.memset(gmask[:, :], 1)
            nc.gpsimd.memset(chunk_start[:, :], 1.0)
            fence(nc.gpsimd.memset(sel4_f, 0.0))
            nc.gpsimd.memset(chunk_start[:, 0:2 * T:CH], 0.0)
            v = cmask[:, P:3 * P].rearrange("p (a n) -> p a n", a=2)
            nc.gpsimd.affine_select(out=v, in_=v, compare_op=ALU.is_ge, fill=-1e30, base=0,
                                    pattern=[[0, 2], [-1, P]], channel_multiplier=1)
            for m in (mmask, gmask):
                for c in (0, 2 * P):
                    v = m[:, c:c + P]
                    nc.gpsimd.affine_select(out=v, in_=v, compare_op=ALU.is_ge, fill=0.0, base=0,
                                            pattern=[[1, P]], channel_multiplier=-1)
            fence(nc.gpsimd.affine_select(out=sel4_f, in_=sel4_f, compare_op=ALU.not_equal, fill=1.0,
                                          base=0, pattern=[[1, 4], [0, P]], channel_multiplier=-1))
            n = 0
            for l in range(L):
                if l:
                    b, k = FILL[l - 1, "acc", 3]
                    pool.wait_ge(full[b], k + 1)
                    pool.dma_start(ws_raw, w_small_d[l]).then_inc(ws_in, 16)
                    pool.dma_start(gw[0:16, :], gate_w[l]).then_inc(ws_in, 16)
                for name, o in UNITS:
                    if name not in BIASED:
                        continue
                    if n >= 3:
                        pl, pname = divmod(n - 3, len(BIASED))
                        b, k = FILL[pl, BIASED[pname], 1]
                        pool.wait_ge(drained[b], k + 1)
                    if n:
                        pool.dma_start(bias[:, n % 3, :], b_in[l, o:o + W].partition_broadcast(P))\
                            .then_inc(bias_in[n % 3], 16)
                    n += 1
                    if name == "mv":
                        b, k = FILL[l, "qkT", 3]
                        pool.wait_ge(full[b], k + 1)
                        nc.gpsimd.memset(conv_in[:, :, 0:3], 0.0).then_inc(pads, 1)
                    if name == "gr":
                        b, k = FILL[l, "s1", 3]
                        pool.wait_ge(full[b], k + 1)
                        nc.gpsimd.memset(g_att, 0.0).then_inc(pads, 1)
            b, k = FILL[L - 1, "g2'", 1]
            pool.wait_ge(drained[b], k + 1)
            made = 0

            def fence2(ins):
                nonlocal made
                ins.then_inc(moe_consts, 1)
                made += 1
                pool.wait_ge(moe_consts, made)

            nc.gpsimd.memset(allones, 1.0)
            nc.gpsimd.memset(zeros, 0.0)
            nc.gpsimd.iota(iota_i, pattern=[[1, P]], base=0, channel_multiplier=0)
            nc.gpsimd.memset(pos[:, :, 16:17], -1.0)
            nc.gpsimd.memset(gmat[:, :, 16:17], 0.0)
            fence2(nc.gpsimd.memset(tri, 1.0))
            fence2(nc.gpsimd.affine_select(out=tri, in_=tri, compare_op=ALU.is_gt, fill=0.0, base=0,
                                           pattern=[[1, P]], channel_multiplier=-1))
            pool.dma_start(rbias, router_b.partition_broadcast(P)).then_inc(fg_in, 16)
            pool.wait_ge(y_ready, 2 * L * NT)
            pool.dma_start(ws_raw[:, 0:KT * E], router_d).then_inc(ws_in, 16)
            pool.dma_start(fin_g, final_g.partition_broadcast(P)).then_inc(fg_in, 16)
            pool.dma_start(ffn_g, ffn_norm_g[L - 1].partition_broadcast(P)).then_inc(fg_in, 16)
            pool.wait_ge(fg_in, 48)

        @block.tensor
        def _(pe):
            mm = nc.tensor.matmul
            for_3 = ((0, 0), (0, 1), (1, 0))
            hT, yT, ws, wsp = (hT_hi, hT_lo), (yT_hi, yT_lo), (ws_hi, ws_lo), (w_hi, w_lo)

            def claim(l, tag, i=0):
                b, k = FILL[l, tag, i]
                if k:
                    pe.wait_ge(drained[b], k)
                return b

            def done(ins, l, tag, i=0):
                ins.then_inc(full[FILL[l, tag, i][0]], 1)

            def await_drained(l, tag, i=0):
                b, k = FILL[l, tag, i]
                pe.wait_ge(drained[b], k + 1)

            def transposes(l, tag, src, half):
                for i in (2 * half, 2 * half + 1):
                    b = claim(l, tag, i)
                    for k in (2 * i, 2 * i + 1):
                        for t in range(NT):
                            ins = nc.tensor.transpose(ps[:, b, (k % 2) * T + t * P:(k % 2) * T + (t + 1) * P],
                                                      src[:, t, k * P:(k + 1) * P], ident[:, :])
                    done(ins, l, tag, i)

            def chunk(l, name, c, left=None, between=None):
                n = LAYER_BASE[l] + CPOS[name, c]
                s = n % RS
                if left:
                    for i in (2 * c, 2 * c + 1):
                        await_drained(l, left, i)
                pe.wait_ge(lo_ready, n + 1)
                if name in FEATURE_MAJOR:
                    for i in range(2):
                        b = FILL[l, name, i][0] if c else claim(l, name, i)
                        for kk in range(4):
                            k = 4 * c + kk
                            for m in (2 * i, 2 * i + 1):
                                for pa, (a, r) in enumerate(for_3):
                                    ins = mm(ps[:, b, (m % 2) * T:(m % 2 + 1) * T],
                                             wsp[a][:, s, kk * W + m * P:kk * W + (m + 1) * P], hT[r][:, k, :],
                                             start=(k == 0 and m % 2 == 0 and pa == 0),
                                             stop=(k == KT - 1 and m % 2 == 1 and pa == 2), skip_group_check=True)
                        if c:
                            done(ins, l, name, i)
                elif name[:2] == "up":
                    for t in range(NT):
                        b = claim(l, name, 2 * c + t)
                        for k in range(4):
                            for pa, (a, r) in enumerate(for_3):
                                ins = mm(ps[:, b, :], yT[a][:, k, t * P:(t + 1) * P], wsp[r][:, s, k * W:(k + 1) * W],
                                         start=(k == 0 and pa == 0), stop=(k == 3 and pa == 2))
                        done(ins, l, name, 2 * c + t)
                    return
                else:
                    for t in range(NT):
                        b = FILL[l, name, t][0] if c else claim(l, name, t)
                        for kk in range(4):
                            k = 4 * c + kk
                            for pa, (a, r) in enumerate(for_3):
                                ins = mm(ps[:, b, :], hT[a][:, k, t * P:(t + 1) * P],
                                         wsp[r][:, s, kk * W:(kk + 1) * W],
                                         start=(k == 0 and pa == 0), stop=(k == KT - 1 and pa == 2))
                        if c:
                            done(ins, l, name, t)
                        if t == 0 and between:
                            between()
                if c == 0:
                    ins.then_inc(w_used, 1)

            def unit(l, name):
                chunk(l, name, 0)
                chunk(l, name, 1)

            def y_transposes(l, br):
                if br:
                    pe.wait_ge(y_ready, (2 * l + br) * NT)
                else:
                    await_drained(l, "pv1", 0)
                    await_drained(l, "pv1", 1)
                for i in range(2):
                    b = claim(l, f"yT{br}", i)
                    for m in range(2):
                        for t in range(NT):
                            ins = nc.tensor.transpose(ps[:, b, m * T + t * P:m * T + (t + 1) * P],
                                                      ytok[:, t, (2 * i + m) * P:(2 * i + m + 1) * P], ident[:, :])
                    done(ins, l, f"yT{br}", i)

            def scores(l, g):
                for hh in range(4):
                    h = 4 * g + hh
                    b = claim(l, f"s{g}", hh)
                    p0 = HD * (h % 2)
                    q, k = qkT[p0:p0 + HD, h // 2, :], qkT[p0:p0 + HD, 4 + h // 2, :]
                    mm(ps[:, b, 0:T], q[:, P:2 * P], k, start=True, stop=True)
                    done(mm(ps[:, b, T:T + P], q[:, 0:P], k[:, 0:P], start=True, stop=True), l, f"s{g}", hh)

            def prob_transposes(l, g):
                pe.wait_ge(p_ready, 2 * l + g + 1)
                for hh in range(4):
                    b = claim(l, f"pT{g}", hh)
                    for j in range(3):
                        ins = nc.tensor.transpose(ps[:, b, j * P:(j + 1) * P], sc[:, g, hh, j * P:(j + 1) * P],
                                                  ident[:, :])
                    done(ins, l, f"pT{g}", hh)

            def prob_values(l, g):
                for hh in range(4):
                    await_drained(l, f"pT{g}", hh)
                b0, b1 = claim(l, f"pv{g}", 0), claim(l, f"pv{g}", 1)
                for hh in range(4):
                    h = 4 * g + hh
                    ins = mm(ps[:, b0, hh * HD:(hh + 1) * HD], pT[:, hh, 2 * P:3 * P], vm[:, 0, h * HD:(h + 1) * HD],
                             start=True, stop=True)
                done(ins, l, f"pv{g}", 0)
                for hh in range(4):
                    h = 4 * g + hh
                    for j in range(2):
                        ins = mm(ps[:, b1, hh * HD:(hh + 1) * HD], pT[:, hh, j * P:(j + 1) * P],
                                 vm[:, j, h * HD:(h + 1) * HD], start=(j == 0), stop=(j == 1))
                done(ins, l, f"pv{g}", 1)

            def gla_scores(l):
                pe.wait_ge(gla_ops, l + 1)
                ki, ke = gB.rearrange("p (m n) -> p m n", m=2), gE.rearrange("p (m n) -> p m n", m=2)
                for h in range(4):
                    b = claim(l, "gs", h)
                    p0, m = GD * (h % 2), h // 2

                    def block_(c, col, lhs, rhs):
                        q0 = CH * (c % 2)
                        return mm(ps[q0:q0 + CH, b, col:col + rhs.shape[1]], lhs[p0:p0 + GD, m, c * CH:(c + 1) * CH],
                                  rhs, start=True, stop=True)
                    qd = gqk[p0:p0 + GD, m, :]
                    for c in range(4):
                        lo_col = 0 if c < 2 else T
                        q_lo = 0 if c < 2 else P
                        if c % 2:
                            block_(c, lo_col, ke, qd[:, q_lo:q_lo + CH])
                        ins = block_(c, lo_col + CH * (c % 2), ki, qd[:, c * CH:(c + 1) * CH])
                        if c < 3:
                            ins = block_(c, lo_col + CH * (c % 2) + CH, ke, qd[:, (c + 1) * CH:(c + 2) * CH])
                        if c == 0:
                            ins = block_(c, P, ke, gx[p0:p0 + GD, m, 0:2 * CH])
                        if c == 1:
                            ins = block_(c, 3 * CH, ke, gx[p0:p0 + GD, m, 2 * CH:3 * CH])
                    done(ins, l, "gs", h)

            def att_values(l, tag, att, v):
                b0, b1 = claim(l, tag, 0), claim(l, tag, 1)
                for h in range(4):
                    ins = mm(ps[:, b0, h * P:(h + 1) * P], att[:, h, 0:P], v[:, 0, h * P:(h + 1) * P],
                             start=True, stop=True)
                done(ins, l, tag, 0)
                for h in range(4):
                    mm(ps[:, b1, h * P:(h + 1) * P], att[:, h, P:2 * P], v[:, 0, h * P:(h + 1) * P],
                       start=True, stop=False)
                    ins = mm(ps[:, b1, h * P:(h + 1) * P], att[:, h, 2 * P:3 * P], v[:, 1, h * P:(h + 1) * P],
                             start=False, stop=True)
                done(ins, l, tag, 1)

            def norm_transposes(l, h):
                if l:
                    for t in range(NT):
                        await_drained(l - 1, "acc", 2 * h + t)
                else:
                    pe.wait_ge(x_in[h], 16 * NT)
                transposes(l, "norm", xt, h)

            def ffn_transposes(l, h):
                for t in range(NT):
                    await_drained(l, ("wo", "wo'")[h], t)
                transposes(l, "fnorm", xt, h)

            pe.wait_ge(consts, 2)
            for h in range(2):
                norm_transposes(0, h)
            for l in range(L):
                chunk(l, "mq", 0, "norm", between=(lambda: norm_transposes(l, 1)) if l else None)
                chunk(l, "mq", 1, "norm")
                chunk(l, "mk", 0)
                pe.wait_ge(rb_ready, l + 1)
                b = claim(l, "rb")
                for t in range(NT):
                    ins = mm(ps[:, b, t * P:(t + 1) * P], rcol[:, t, :], ident[:, :], start=True, stop=True)
                done(ins, l, "rb")
                chunk(l, "mk", 1)
                pe.wait_ge(ws_ready, l + 1)
                b = claim(l, "small")
                for k in range(KT):
                    for pa, (a, r) in enumerate(for_3):
                        ins = mm(ps[0:SW, b, 0:T], ws[a][:, k * SW:(k + 1) * SW], hT[r][:, k, :],
                                 start=(k == 0 and pa == 0), stop=(k == KT - 1 and pa == 2))
                done(ins, l, "small")
                unit(l, "mv")
                pe.wait_ge(rope_done, l + 1)
                for i in range(4):
                    b = claim(l, "qkT", i)
                    for m in range(2):
                        for t in range(NT):
                            ins = nc.tensor.transpose(ps[:, b, m * T + t * P:m * T + (t + 1) * P],
                                                      zqk[:, t, (2 * i + m) * P:(2 * i + m + 1) * P], ident[:, :])
                    done(ins, l, "qkT", i)
                unit(l, "gqk")
                unit(l, "gv")
                for i in range(4):
                    await_drained(l, "qkT", i)
                scores(l, 0)
                unit(l, "gr")
                scores(l, 1)
                unit(l, "lq")
                b = claim(l, "ga")
                pe.wait_ge(ws_in, 32 * (l + 1))
                await_drained(l, "small")
                for m in range(2):
                    ins = mm(ps[:, b, m * T:(m + 1) * T], gw[0:16, m * P:(m + 1) * P], aT[0:16, :],
                             start=True, stop=True)
                done(ins, l, "ga")
                unit(l, "lk")
                prob_transposes(l, 0)
                unit(l, "lv")
                prob_values(l, 0)
                prob_transposes(l, 1)
                unit(l, "lo")
                prob_values(l, 1)
                unit(l, "g0")
                pe.wait_ge(rows_ready, l + 1)
                pe.wait_ge(floors, l + 1)
                b = claim(l, "lc")
                for i, r in enumerate((gl, fls)):
                    for t in range(NT):
                        ins = nc.tensor.transpose(ps[:, b, 8 * i + 4 * t:8 * i + 4 * t + 4],
                                                  r[0:4, t * P:(t + 1) * P], ident[0:4, 0:4])
                done(ins, l, "lc")
                gla_scores(l)
                chunk(l, "g0'", 0)
                y_transposes(l, 0)
                chunk(l, "g0'", 1)
                for i in range(4):
                    await_drained(l, "gs", i)
                await_drained(l, "gv", 1)
                att_values(l, "go", g_att, vg)
                for i in range(2):
                    b = claim(l, "mb", i)
                    for hh in range(2):
                        for m in (rmax_hi, rmax_lo):
                            ins = mm(ps[:, b, hh * T:(hh + 1) * T], sel4[0:4, 2 * i + hh, :], m[0:4, :],
                                     start=(m is rmax_hi), stop=(m is rmax_lo))
                    done(ins, l, "mb", i)
                for i in range(2):
                    await_drained(l, "yT0", i)
                unit(l, "up0")
                chunk(l, "g1", 0)
                y_transposes(l, 1)
                chunk(l, "g1", 1)
                pe.wait_ge(mqk_ready, 2 * (l + 1))
                for h in range(4):
                    b = claim(l, "ms", h)
                    mm(ps[:, b, 0:T], mqk[:, 4 + h, 0:P], mqk[:, h, :], start=True, stop=True)
                    done(mm(ps[:, b, T:T + P], mqk[:, 4 + h, P:2 * P], mqk[:, h, P:2 * P], start=True, stop=True),
                         l, "ms", h)
                unit(l, "g1'")
                for i in range(2):
                    await_drained(l, "yT1", i)
                unit(l, "up1")
                for i in range(4):
                    await_drained(l, "ms", i)
                await_drained(l, "lv", 1)
                att_values(l, "mo", mW, vl)
                b = claim(l, "mo", 2)
                for h in range(4):
                    mm(ps[:, b, h:h + 1], mW[:, h, 0:P], ones[:, 0:1], start=True, stop=True)
                    mm(ps[:, b, 4 + h:5 + h], mW[:, h, P:2 * P], ones[:, 0:1], start=True, stop=False)
                    ins = mm(ps[:, b, 4 + h:5 + h], mW[:, h, 2 * P:3 * P], ones[:, 0:1], start=False, stop=True)
                done(ins, l, "mo", 2)
                unit(l, "g2")
                y_transposes(l, 2)
                chunk(l, "g2'", 0)
                for i in range(2):
                    await_drained(l, "yT2", i)
                chunk(l, "up2", 0)
                chunk(l, "g2'", 1)
                pe.wait_ge(merged_ready, 2 * l + 1)
                transposes(l, "mgT", xn, 0)
                chunk(l, "up2", 1)
                chunk(l, "wo", 0, "mgT")
                pe.wait_ge(merged_ready, 2 * l + 2)
                transposes(l, "mgT", xn, 1)
                chunk(l, "wo'", 0)
                chunk(l, "wo", 1, "mgT")
                chunk(l, "wo'", 1, between=lambda: ffn_transposes(l, 0))
                if l:
                    ffn_transposes(l, 1)
                if l == 0:
                    def hidden_T(i):
                        for t in range(NT):
                            await_drained(0, f"gu{i}", t)
                        b = claim(0, f"hT{i}")
                        for m in range(2):
                            for t in range(NT):
                                ins = nc.tensor.transpose(ps[:, b, m * T + t * P:m * T + (t + 1) * P],
                                                          hid[:, t, m * P:(m + 1) * P], ident[:, :])
                        done(ins, 0, f"hT{i}")

                    for n, (kind, i, c) in enumerate(FF):
                        g = 2 * NU + n
                        if kind == "dn":
                            await_drained(0, f"hT{i}")
                        elif i == 0:
                            for q in (2 * c, 2 * c + 1):
                                await_drained(0, "fnorm", q)
                        pe.wait_ge(lo_ready, g + 1)
                        s = g % RS
                        if kind == "gu":
                            for t in range(NT):
                                b = claim(0, f"gu{i}", t) if c == 0 else FILL[0, f"gu{i}", t][0]
                                for kk in range(4):
                                    k = 4 * c + kk
                                    for pa, (a, r) in enumerate(for_3):
                                        ins = mm(ps[:, b, :], hT[a][:, k, t * P:(t + 1) * P],
                                                 wsp[r][:, s, kk * W:(kk + 1) * W],
                                                 start=(k == 0 and pa == 0), stop=(k == KT - 1 and pa == 2))
                                if c:
                                    done(ins, 0, f"gu{i}", t)
                                if n == 0 and t == 0:
                                    ffn_transposes(0, 1)
                        else:
                            for h in range(2):
                                for t in range(NT):
                                    q = 2 * h + t
                                    b = claim(0, "acc", q) if i == 0 else FILL[0, "acc", q][0]
                                    for kk in range(2):
                                        for pa, (a, r) in enumerate(for_3):
                                            ins = mm(ps[:, b, :], yT[a][:, 2 * (i % 2) + kk, t * P:(t + 1) * P],
                                                     wsp[r][:, s, kk * D + h * W:kk * D + (h + 1) * W],
                                                     start=(i == 0 and kk == 0 and pa == 0),
                                                     stop=(i == NF - 1 and kk == 1 and pa == 2))
                                    if i == NF - 1:
                                        done(ins, 0, "acc", q)
                                    if i == NF - 1 and q == 2:
                                        norm_transposes(1, 0)
                        if USED[g][0] == "w":
                            ins.then_inc(w_used, 1)
                        if kind == "dn" and i + 1 < NF or (kind, i, c) == ("gu", 1, 0):
                            hidden_T(i + 1 if kind == "dn" else 0)

            pe.wait_ge(ws_ready, L + 1)
            b = claim(1, "logits")
            for k in range(KT):
                if k % 2 == 0:
                    await_drained(L - 1, "fnorm", k // 2)
                for pa, (a, r) in enumerate(for_3):
                    ins = mm(ps[0:E, b, 0:T], ws[a][:, k * E:(k + 1) * E], hT[r][:, k, :],
                             start=(k == 0 and pa == 0), stop=(k == KT - 1 and pa == 2))
            done(ins, 1, "logits")
            await_drained(1, "logits")
            b = claim(1, "lgT")
            for t in range(NT):
                ins = nc.tensor.transpose(ps[:, b, t * E:(t + 1) * E], lgT[:, t * P:(t + 1) * P], ident[0:E, 0:E])
            done(ins, 1, "lgT")
            pe.wait_ge(moe_consts, 2)
            pe.wait_ge(ind_ready, 1)
            b = claim(1, "rank")
            mm(ps[:, b, 0:E], tri, ind[:, 0, :], start=True, stop=True)
            mm(ps[:, b, E:2 * E], allones, ind[:, 0, :], start=True, stop=False)
            mm(ps[:, b, E:2 * E], tri, ind[:, 1, :], start=False, stop=True)
            mm(ps[:, b, 2 * E:3 * E], allones, ind[:, 0, :], start=True, stop=False)
            done(mm(ps[:, b, 2 * E:3 * E], allones, ind[:, 1, :], start=False, stop=True), 1, "rank")

            def gather(banks, waits):
                for i in range(2):
                    pe.wait_ge(drained[banks[i]], waits[i])
                    for kk in range(4):
                        k = 4 * i + kk
                        for t in range(NT):
                            ins = mm(ps[:, banks[i], kk * P:(kk + 1) * P], xn[:, t, k * P:(k + 1) * P], sel[:, t, :],
                                     start=(t == 0), stop=(t == NT - 1))
                    ins.then_inc(full[banks[i]], 1)

            def scatter(t, fill):
                for h in range(2):
                    b, k = fill(h)
                    pe.wait_ge(drained[b], k)
                    for y in (ysb_hi, ysb_lo):
                        ins = mm(ps[:, b, :], selT[:, t, :], y[:, 4 * h:4 * h + 4, :], start=(y is ysb_hi),
                                 stop=(y is ysb_lo))
                    ins.then_inc(full[b], 1)

            def moe_pass(pas):
                base = PASS_FILL[pas]
                pe.wait_ge(sel_ready, pas * (E + 1) + 1)
                gather((6, 7), (base[6], base[7]))
                with pe.Fori(0, E) as e:
                    def bank(tag, i=0):
                        b, k = moe_fill(pas, e, tag, i)
                        pe.wait_ge(drained[b], k)
                        return b

                    def hidden_T(i):
                        b, k = moe_fill(pas, e, f"gu{i}", 0)
                        pe.wait_ge(drained[b], k + 1)
                        b = bank(f"hT{i}")
                        for m in range(2):
                            ins = nc.tensor.transpose(ps[:, b, m * P:(m + 1) * P], hid[:, i % 2, m * P:(m + 1) * P],
                                                      ident[:, :])
                        ins.then_inc(full[b], 1)

                    for n, (kind, i, c) in enumerate(FF):
                        if n < 2:
                            pe.wait_ge(drained[6 + n], base[6 + n] + PRO[6 + n] + e * nexp[6 + n])
                        if n == FFC - 1:
                            pe.wait_ge(sel_ready, pas * (E + 1) + 2 + e)
                            fb = [moe_fill(pas, e, "gather", q) for q in range(2)]
                            gather([f[0] for f in fb], [f[1] for f in fb])
                        if kind == "dn":
                            b, k = moe_fill(pas, e, f"hT{i}", 0)
                            pe.wait_ge(drained[b], k + 1)
                        pe.wait_ge(lo_ready, e * FFC + (MOE_BASE + pas * E * FFC + n + 1))
                        s = n % RS
                        if kind == "gu":
                            b = bank(f"gu{i}") if c == 0 else EXPERT[f"gu{i}", 0][0]
                            for kk in range(4):
                                k = 4 * c + kk
                                for pa, (a, r) in enumerate(for_3):
                                    ins = mm(ps[:, b, :], hT[a][:, k, 0:P], wsp[r][:, s, kk * W:(kk + 1) * W],
                                             start=(k == 0 and pa == 0), stop=(k == KT - 1 and pa == 2))
                            if c:
                                ins.then_inc(full[b], 1)
                        else:
                            for h in range(2):
                                b = bank("acc", h) if i == 0 else EXPERT["acc", h][0]
                                for kk in range(2):
                                    for pa, (a, r) in enumerate(for_3):
                                        ins = mm(ps[:, b, :], yT[a][:, 2 * (i % 2) + kk, 0:P],
                                                 wsp[r][:, s, kk * D + h * W:kk * D + (h + 1) * W],
                                                 start=(i == 0 and kk == 0 and pa == 0),
                                                 stop=(i == NF - 1 and kk == 1 and pa == 2))
                                if i == NF - 1:
                                    ins.then_inc(full[b], 1)
                        if EUSED[n][0] == "w":
                            ins.then_inc(w_used, 1)
                        if (kind, i, c) == ("gu", 1, 0):
                            pe.wait_ge(zeroed, pas + 1)
                            for q in (3, 4, 5):
                                pe.wait_ge(drained[q], base[q] + e * nexp[q])
                            scatter(0, lambda h: moe_fill(pas, e, "sc0", h))
                        if (kind, i, c) == ("gu", 2, 0):
                            scatter(1, lambda h: moe_fill(pas, e, "sc1", h))
                        if kind == "dn" and i + 1 < NF or (kind, i, c) == ("gu", 1, 0):
                            hidden_T(i + 1 if kind == "dn" else 0)
                        if kind == "dn" and i == 4:
                            b = bank("selT")
                            for t in range(NT):
                                nc.tensor.transpose(ps[:, b, t * P:(t + 1) * P], sel[:, t, :], ident[:, :])
                            for t in range(NT):
                                ins = mm(ps[:, b, T:T + 1], sel[:, t, :], gcur[:, t:t + 1], start=(t == 0),
                                         stop=(t == NT - 1))
                            ins.then_inc(full[b], 1)
                for q in (3, 4, 5):
                    pe.wait_ge(drained[q], base[q] + E * nexp[q])
                for t in range(NT):
                    scatter(t, lambda h: (6 + h, base[6 + h] + PRO[6] + E * nexp[6 + h] + t))

            moe_pass(0)
            many = pe.value_load(cnt_i[0:1, 0:1], min_val=0, max_val=T)
            with pe.If(many > P):
                moe_pass(1)

        @block.scalar
        def _(act):
            copy, A = nc.scalar.copy, nc.scalar.activation
            seq, nsplit, norms = [0], [0], [0]

            def link(ins):
                seq[0] += 1
                ins.then_inc(act_seq, 1)
                act.wait_ge(act_seq, seq[0])

            def await_full(l, tag, i=0):
                b, k = FILL[l, tag, i]
                act.wait_ge(full[b], k + 1)
                return b

            def await_drained(l, tag, i=0):
                b, k = FILL[l, tag, i]
                act.wait_ge(drained[b], k + 1)

            def split_to(n):
                while nsplit[0] <= min(n, MOE_BASE - 1):
                    g = nsplit[0]
                    act.wait_ge(raw_in[g % RM], 32 * (g // RM + 1))
                    if g >= RS:
                        act.wait_ge(*last_use(g - RS))
                    copy(w_hi[:, g % RS, :], slot_raw(g, False)).then_inc(hi_ready, 1)
                    nsplit[0] += 1

            def ahead(l, name, c=1):
                split_to(LAYER_BASE[l] + CPOS[name, c] + 2)

            def squares(h):
                for t in range(NT):
                    c = slice(h * W, (h + 1) * W)
                    A(xn[:, t, c], xt[:, t, c], ACT.Square, accum_out=(ss, ss1)[h][:, t:t + 1]).then_inc(stat, 1)

            def load_sqrt():
                A(idle, ones[:, 0:2], ACT.Sqrt)

            def norm_stats():
                q = norms[0]
                norms[0] += 1
                act.wait_ge(statv, q + 1)
                A(nt0, var, ACT.Sqrt).then_inc(stat, 1)

            def hi_of(l, tag, i, dst, gain=None):
                b = await_full(l, tag, i)
                if gain is None:
                    copy(dst[:, 2 * i:2 * i + 2, :], ps[:, b, :].rearrange("p (m n) -> p m n", m=2))\
                        .then_inc(hi_part, 1)
                    return
                for m in range(2):
                    k = 2 * i + m
                    ins = A(dst[:, k, :], ps[:, b, m * T:(m + 1) * T], ACT.Copy,
                            scale=cols[:, l, gain + k:gain + k + 1])
                ins.then_inc(hi_part, 1)

            def sigmoid_gates(l, name):
                b, h = int(name[1]), int(name.endswith("'"))
                for t in range(NT):
                    await_drained(l, name, t)
                    A(gates[:, h, t, :], gates[:, h, t, :], ACT.Sigmoid).then_inc(gate_ready, 1)

            def conv_head(l, name):
                u = 4 * (name == "lk")
                for i in range(2):
                    await_drained(l, name, i)
                for m in range(4):
                    v = conv_in[:, u + m, 3:3 + T]
                    ins = A(v, v, ACT.Identity, bias=cols[:, l, C_BL + u + m:C_BL + u + m + 1])
                link(ins)
                for m in range(4):
                    c = C_CW + 4 * (u + m)
                    ins = A(mqk[:, u + m, :], conv_in[:, u + m, 0:T], ACT.Identity, scale=cols[:, l, c:c + 1],
                            bias=cols[:, l, C_CB + u + m:C_CB + u + m + 1])
                ins.then_inc(conv0, 1)

            act.wait_ge(consts, 2)
            A(y0, ident[:, 0:2], ACT.Copy)
            act.wait_ge(c_in, 16)
            for l in range(L):
                for i in range(2):
                    hi_of(l, "norm", i, hT_hi, C_AG)
                split_to(LAYER_BASE[l])
                if l:
                    load_sqrt()
                for i in range(2, 4):
                    hi_of(l, "norm", i, hT_hi, C_AG)
                split_to(LAYER_BASE[l] + 1)
                squares(0)
                squares(1)
                ahead(l, "mq", 0)
                norm_stats()
                act.wait_ge(ws_in, 32 * (l + 1))
                if l:
                    await_full(l - 1, "acc", 3)
                copy(ws_hi[:, 0:KT * SW], ws_raw).then_inc(ws_hi_ready, 1)
                ahead(l, "mq")
                ahead(l, "mk")
                ahead(l, "mv")
                for i in range(2):
                    b = await_full(l, "qkT", i)
                    copy(qkT[:, 2 * i:2 * i + 2, :], ps[:, b, :].rearrange("p (m n) -> p m n", m=2))\
                        .then_inc(drained[b], 1)
                ahead(l, "gqk")
                ahead(l, "gv")
                act.wait_ge(sub_ready, 2 * l + 1)
                A(sc[:, 0, :, :], sc[:, 0, :, :], ACT.Exp, scale=HD ** -0.5).then_inc(p_ready, 1)
                ahead(l, "gr")
                act.wait_ge(sub_ready, 2 * l + 2)
                A(sc[:, 1, :, :], sc[:, 1, :, :], ACT.Exp, scale=HD ** -0.5).then_inc(p_ready, 1)
                ahead(l, "lq")
                conv_head(l, "lq")

                def probs_out(g):
                    for hh in (0, 2):
                        b = await_full(l, f"pT{g}", hh)
                        copy(pT[:, hh, :], ps[:, b, 0:384]).then_inc(drained[b], 1)

                ahead(l, "lk")
                conv_head(l, "lk")
                probs_out(0)
                ahead(l, "lv", 0)
                await_full(l, "pT0", 3)
                await_drained(l, "ga")
                await_drained(l, "small")
                A(gB, gz, ACT.Abs)
                link(A(cumf[0:4, :], fT[0:4, :], ACT.Abs))
                A(gB, gB, ACT.Exp, scale=-1.0)
                link(A(cumf[0:4, :], cumf[0:4, :], ACT.Exp, scale=-1.0))
                A(gB, gB, ACT.Ln, bias=1.0)
                A(cumf[0:4, :], cumf[0:4, :], ACT.Ln, bias=1.0).then_inc(lsg2, 1)
                ahead(l, "lv")
                probs_out(1)
                ahead(l, "lo", 0)
                act.wait_ge(gla_cum, l + 1)
                A(gA, gC, ACT.Exp, scale=1.0 / TAU)
                A(gB, gC, ACT.Exp, scale=-1.0 / TAU)
                A(gE, gE, ACT.Exp, scale=1.0 / TAU).then_inc(gla_exp, 1)
                act.wait_ge(rows_ready, l + 1)
                A(fls[0:4, :], fls[0:4, :], ACT.Exp, scale=-1.0).then_inc(floors, 1)
                ahead(l, "lo")
                for i in range(2):
                    await_drained(l, "gr", i)
                A(gr, gr, ACT.Silu).then_inc(gate_ready, 1)
                for u in range(2):
                    act.wait_ge(conv3, 2 * l + u + 1)
                    A(mqk[:, 4 * u:4 * u + 4, :], mqk[:, 4 * u:4 * u + 4, :], ACT.Silu).then_inc(mqk_ready, 1)
                for i in range(2):
                    await_drained(l, "lo", i)
                A(lo, lo, ACT.Sigmoid).then_inc(gate_ready, 1)
                ahead(l, "g0")
                sigmoid_gates(l, "g0")
                ahead(l, "g0'", 0)
                for i in range(2):
                    hi_of(l, "yT0", i, yT_hi)
                ahead(l, "g0'", 1)
                sigmoid_gates(l, "g0'")
                for t in range(NT):
                    b = await_full(l, "go", t)
                    A(tmp[:, t * W:(t + 1) * W], ps[:, b, :], ACT.Square).then_inc(gstat, 1)
                ahead(l, "up0", 0)
                act.wait_ge(gstatv, l + 1)
                A(gn0, gvar, ACT.Sqrt).then_inc(gstat, 1)
                ahead(l, "up0")
                await_drained(l, "mb", 1)
                A(mE, mE, ACT.Exp, scale=-1.0).then_inc(mEr, 1)
                ahead(l, "g1", 0)
                for i in range(2):
                    hi_of(l, "yT1", i, yT_hi, C_GN)
                ahead(l, "g1")
                sigmoid_gates(l, "g1")
                ahead(l, "g1'")
                sigmoid_gates(l, "g1'")
                ahead(l, "up1")
                ahead(l, "g2")
                sigmoid_gates(l, "g2")
                for i in range(2):
                    hi_of(l, "yT2", i, yT_hi)
                ahead(l, "g2'", 0)
                ahead(l, "up2", 0)
                ahead(l, "g2'", 1)
                sigmoid_gates(l, "g2'")
                for i in range(2):
                    hi_of(l, "mgT", i, hT_hi)
                ahead(l, "up2", 1)
                ahead(l, "wo", 0)
                for i in range(2, 4):
                    hi_of(l, "mgT", i, hT_hi)
                if l == L - 1:
                    act.wait_ge(ws_in, 32 * L + 16)
                    copy(ws_hi[:, 0:KT * E], ws_raw[:, 0:KT * E]).then_inc(ws_hi_ready, 1)
                ahead(l, "wo", 1)
                for i in range(2):
                    hi_of(l, "fnorm", i, hT_hi, C_FG)
                ahead(l, "wo'", 1)
                for t in range(NT):
                    await_drained(l, "wo", t)
                squares(0)
                load_sqrt()
                for i in range(2, 4):
                    hi_of(l, "fnorm", i, hT_hi, C_FG)
                for t in range(NT):
                    await_drained(l, "wo'", t)
                squares(1)
                if l == L - 1:
                    b = await_full(1, "logits")
                    copy(lgT, ps[0:E, b, 0:T]).then_inc(drained[b], 1)
                norm_stats()
                if l == 0:
                    for n, (kind, i, c) in enumerate(FF):
                        if n != 1:
                            split_to(2 * NU + n + 2)
                        if kind == "gu" and c == 1:
                            act.wait_ge(rstd_ready, 2)
                            for t in range(NT):
                                b = await_full(0, f"gu{i}", t)
                                A(silu_g[:, t, :], ps[:, b, 0:256], ACT.Silu, scale=rstds[:, 1, t:t + 1])\
                                    .then_inc(silu_ready, 1)
                        if kind == "dn" and i + 1 < NF or (kind, i, c) == ("gu", 1, 0):
                            i = i + 1 if kind == "dn" else 0
                            b = await_full(0, f"hT{i}")
                            copy(yT_hi[:, 2 * (i % 2):2 * (i % 2) + 2, :],
                                 ps[:, b, :].rearrange("p (m n) -> p m n", m=2)).then_inc(hi_part, 1)

            def split_moe(pas, e, j):
                act.wait_ge(moe_in[j % RE], e * (32 * FFC // RE) + 32 * (pas * E * FFC // RE + j // RE + 1))
                if j < 2 and pas == 0:
                    act.wait_ge(*last_use(MOE_BASE + j - RS))
                elif j < 2:
                    act.wait_ge(*moe_last_use(pas - 1, E - 1, FFC + j - RS))
                elif j - RS < FFC:
                    act.wait_ge(*moe_last_use(pas, e, j - RS))
                copy(w_hi[:, j % RS, :], slot_raw(j, True)).then_inc(hi_ready, 1)

            act.wait_ge(router_d2, 1)
            A(g12[:, :, 0:1], g12[:, :, 0:1], ACT.Exp).then_inc(router_e, 1)
            for j in range(2):
                split_moe(0, 0, j)

            def gather_hi(banks, waits):
                for i in range(2):
                    act.wait_ge(full[banks[i]], waits[i])
                    copy(hT_hi[:, 4 * i:4 * i + 4, 0:P], ps[:, banks[i], :].rearrange("p (m n) -> p m n", m=4))\
                        .then_inc(hi_part, 1)

            def moe_pass(pas):
                base = PASS_FILL[pas]
                if pas:
                    for j in range(2):
                        split_moe(pas, 0, j)
                gather_hi((6, 7), (base[6] + 1, base[7] + 1))

                def expert(e, first, end, last):
                    def moe_full(tag, i=0):
                        b, k = moe_fill(pas, e, tag, i)
                        act.wait_ge(full[b], k + 1)
                        return b

                    for n, (kind, i, c) in enumerate(FF):
                        if not first <= n < end:
                            continue
                        if n + 2 < FFC or not last:
                            split_moe(pas, e, n + 2)
                        if n == FFC - 1:
                            fb = [moe_fill(pas, e, "gather", q) for q in range(2)]
                            gather_hi([f[0] for f in fb], [f[1] + 1 for f in fb])
                            b, k = moe_fill(pas, e, "selT", 0)
                            act.wait_ge(drained[b], k + 1)
                            for h in range(2):
                                b = moe_full("acc", h)
                                A(ysb_hi[:, 4 * h:4 * h + 4, :], ps[:, b, :].rearrange("p (m n) -> p m n", m=4),
                                  ACT.Copy, scale=gslot).then_inc(hi_part, 1)
                        if kind == "gu" and c == 1:
                            b = moe_full(f"gu{i}")
                            A(silu_g[:, i % 2, :], ps[:, b, 0:256], ACT.Silu).then_inc(silu_ready, 1)
                        if kind == "dn" and i + 1 < NF or (kind, i, c) == ("gu", 1, 0):
                            i = i + 1 if kind == "dn" else 0
                            b = moe_full(f"hT{i}")
                            copy(yT_hi[:, 2 * (i % 2):2 * (i % 2) + 2, 0:P],
                                 ps[:, b, 0:2 * P].rearrange("p (m n) -> p m n", m=2)).then_inc(hi_part, 1)

                seam = 3 * (NF // 2)
                expert(0, 0, seam, False)
                with act.Fori(0, E - 1) as e:
                    expert(e, seam, FFC, False)
                    expert(e + 1, 0, seam, False)
                expert(E - 1, seam, FFC, True)

            moe_pass(0)
            many = act.value_load(cnt_i[0:1, 0:1], min_val=0, max_val=T)
            with act.If(many > P):
                moe_pass(1)
            load_sqrt()
            for h in range(2):
                for t in range(NT):
                    act.wait_ge(final_rows, NT * h + t + 1)
                    scratch = ytok[:, h, :] if t == 0 else tmp[:, h * W:(h + 1) * W]
                    A(scratch, xt[:, t, h * W:(h + 1) * W], ACT.Square, accum_out=(ss, ss1)[h][:, t:t + 1])\
                        .then_inc(stat, 1)
            norm_stats()
            act.wait_ge(rfin_ready, 1)
            for h in range(2):
                c = slice(h * W, (h + 1) * W)
                A(xn[:, 1, c], xn[:, 1, c], ACT.Copy, scale=rfin[:, 1:2]).then_inc(scaled[1], 1)

        @block.vector
        def _(dve):
            V = nc.vector
            tt, ts, stt = V.tensor_tensor, V.tensor_scalar, V.scalar_tensor_tensor
            seq, nsplit, nhi, nb, nnorm, nsilu = [0], [0], [0], [0], [0], [0]

            def note(ins):
                seq[0] += 1
                ins.then_inc(dve_seq, 1)

            def settle():
                dve.wait_ge(dve_seq, seq[0])

            def link(ins):
                note(ins)
                settle()

            def await_full(l, tag, i=0):
                b, k = FILL[l, tag, i]
                dve.wait_ge(full[b], k + 1)
                return b

            def await_drained(l, tag, i=0):
                b, k = FILL[l, tag, i]
                dve.wait_ge(drained[b], k + 1)

            def split_to(n):
                while nsplit[0] <= min(n, MOE_BASE - 1):
                    g = nsplit[0]
                    dve.wait_ge(hi_ready, g + 1)
                    tt(w_lo[:, g % RS, :], slot_raw(g, False), w_hi[:, g % RS, :], ALU.subtract)\
                        .then_inc(lo_ready, 1)
                    nsplit[0] += 1

            def ahead(l, name, c=1):
                split_to(LAYER_BASE[l] + CPOS[name, c] + 2)

            def rsqrt(y, v, t0, r):
                link(V.reciprocal(y, t0))
                link(tt(t0, y, y, ALU.mult))
                link(tt(t0, t0, v, ALU.mult))
                link(ts(t0, t0, -0.5, 1.5, ALU.mult, ALU.add))
                link(tt(r, y, t0, ALU.mult))

            def norm(r, ready=None):
                q = nnorm[0]
                nnorm[0] += 1
                dve.wait_ge(stat, 5 * q + 2)
                link(ts(var0, ss, 1.0 / D, EPS, ALU.mult, ALU.add))
                dve.wait_ge(stat, 5 * q + 4)
                stt(var, ss1, 1.0 / D, var0, ALU.mult, ALU.add).then_inc(statv, 1)
                dve.wait_ge(statv, q + 1)
                dve.wait_ge(stat, 5 * q + 5)
                link(V.reciprocal(y0, nt0))
                link(tt(nt0, y0, y0, ALU.mult))
                link(tt(nt0, nt0, var, ALU.mult))
                link(ts(nt0, nt0, -0.5, 1.5, ALU.mult, ALU.add))
                tt(r, y0, nt0, ALU.mult).then_inc(ready or rstd_ready, 1)
                dve.wait_ge(ready or rstd_ready, 1 if ready else q + 1)

            def lo_of(l, tag, i, dst_hi, dst_lo, gain=None):
                b = await_full(l, tag, i)
                nhi[0] += 1
                dve.wait_ge(hi_part, nhi[0])
                if gain is None:
                    ins = tt(dst_lo[:, 2 * i:2 * i + 2, :], ps[:, b, :].rearrange("p (m n) -> p m n", m=2),
                             dst_hi[:, 2 * i:2 * i + 2, :], ALU.subtract)
                else:
                    for m in range(2):
                        k = 2 * i + m
                        ins = stt(dst_lo[:, k, :], ps[:, b, m * T:(m + 1) * T], cols[:, l, gain + k:gain + k + 1],
                                  dst_hi[:, k, :], ALU.mult, ALU.subtract)
                ins.then_inc(drained[b], 1)

            def biased(l, name, dst):
                s = nb[0] % 3
                dve.wait_ge(bias_in[s], 16 * (nb[0] // 3 + 1))
                nb[0] += 1
                for t in range(NT):
                    b = await_full(l, name, t)
                    stt(dst(t), ps[:, b, :], rstds[:, 2 * l, t:t + 1], bias[:, s, :], ALU.mult, ALU.add)\
                        .then_inc(drained[b], 1)

            def merge(l, br, h):
                dve.wait_ge(gate_ready, NG * l + GATES[f"g{br}" + "'" * h])
                for t in range(NT):
                    b = await_full(l, f"up{br}", 2 * h + t)
                    dst = gates[:, h, t, :] if br else xn[:, t, h * W:(h + 1) * W]
                    tt(dst, ps[:, b, :], gates[:, h, t, :], ALU.mult).then_inc(drained[b], 1)
                if br:
                    for t in range(NT):
                        await_drained(l, f"up{br}", 2 * h + t)
                        m = xn[:, t, h * W:(h + 1) * W]
                        ins = tt(m, m, gates[:, h, t, :], ALU.add)
                        if br == 2 and t == NT - 1:
                            ins.then_inc(merged_ready, 1)
                        else:
                            note(ins)
                    settle()

            def soft_scores(l, g):
                for hh in range(4):
                    b = await_full(l, f"s{g}", hh)
                    tt(sc[:, g, hh, :], ps[:, b, 0:384], cmask[:, :], ALU.add).then_inc(drained[b], 1)
                for hh in range(4):
                    await_drained(l, f"s{g}", hh)
                note(V.reduce_max(mx[:, g, 1, :], sc[:, g, :, 0:T], AX))
                link(V.reduce_max(mx[:, g, 0, :], sc[:, g, :, T:T + P], AX))
                note(tt(sc[:, g, :, 0:T], sc[:, g, :, 0:T], mx[:, g, 1, :].unsqueeze(2).to_broadcast([P, 4, T]),
                        ALU.subtract))
                tt(sc[:, g, :, T:T + P], sc[:, g, :, T:T + P], mx[:, g, 0, :].unsqueeze(2).to_broadcast([P, 4, P]),
                   ALU.subtract).then_inc(sub_ready, 1)

            def row_sums(l, g):
                dve.wait_ge(p_ready, 2 * l + g + 1)
                note(V.reduce_sum(sums[:, g, 1, :], sc[:, g, :, 0:T], AX))
                link(V.reduce_sum(sums[:, g, 0, :], sc[:, g, :, T:T + P], AX))
                note(V.reciprocal(sums[:, g, :, :], sums[:, g, :, :]))

            def probs_out(l, g):
                for hh in (1, 3):
                    b = await_full(l, f"pT{g}", hh)
                    V.tensor_copy(pT[:, hh, :], ps[:, b, 0:384]).then_inc(drained[b], 1)

            def moba_rows(l, g):
                settle()
                for t in range(NT):
                    b = await_full(l, f"pv{g}", t)
                    tt(ytok[:, t, g * T:(g + 1) * T].rearrange("p (h n) -> p h n", h=4),
                       ps[:, b, 0:T].rearrange("p (h n) -> p h n", h=4),
                       sums[:, g, t, :].unsqueeze(2).to_broadcast([P, 4, HD]), ALU.mult).then_inc(drained[b], 1)

            def conv_rows(l, name):
                u = 4 * (name == "lk")
                dve.wait_ge(pads, 2 * l + 1)
                for i in range(2):
                    b = await_full(l, name, i)
                    tt(conv_in[:, u + 2 * i:u + 2 * i + 2, 3:3 + T], ps[:, b, :].rearrange("p (m n) -> p m n", m=2),
                       rb.unsqueeze(1).to_broadcast([P, 2, T]), ALU.mult).then_inc(drained[b], 1)

            def conv_taps(l, u):
                dve.wait_ge(conv0, 2 * l + u + 1)
                for i in range(1, 4):
                    for m in range(4 * u, 4 * u + 4):
                        c = C_CW + 4 * m + i
                        ins = stt(mqk[:, m, :], conv_in[:, m, i:i + T], cols[:, l, c:c + 1], mqk[:, m, :],
                                  ALU.mult, ALU.add)
                        if i < 3:
                            note(ins)
                        elif m % 4 == 3:
                            ins.then_inc(conv3, 1)
                        else:
                            note(ins)
                    settle()

            def small_parts(n, width):
                dve.wait_ge(ws_hi_ready, n)
                tt(ws_lo[:, 0:width], ws_raw[:, 0:width], ws_hi[:, 0:width], ALU.subtract).then_inc(ws_ready, 1)

            dve.wait_ge(c_in, 16)
            for l in range(L):
                for i in range(2):
                    lo_of(l, "norm", i, hT_hi, hT_lo, C_AG)
                split_to(LAYER_BASE[l])
                if l:
                    for t in range(NT):
                        b = await_full(0, "acc", 2 + t)
                        tt(xt[:, t, W:D], xt[:, t, W:D], ps[:, b, :], ALU.add).then_inc(drained[b], 1)
                for i in range(2, 4):
                    lo_of(l, "norm", i, hT_hi, hT_lo, C_AG)
                split_to(LAYER_BASE[l] + 1)
                ahead(l, "mq", 0)
                norm(rstds[:, 2 * l, :])
                for t in range(NT):
                    ins = V.tensor_copy(rcol[:, t, :], rstds[:, 2 * l, t:t + 1].to_broadcast([P, P]))
                ins.then_inc(rb_ready, 1)
                small_parts(l + 1, KT * SW)
                ahead(l, "mq")
                biased(l, "mq", lambda t: zqk[:, t, 0:MIX])
                ahead(l, "mk", 0)
                b = await_full(l, "rb")
                V.tensor_copy(rb, ps[:, b, 0:T]).then_inc(drained[b], 1)
                ahead(l, "mk")
                biased(l, "mk", lambda t: zqk[:, t, MIX:2 * MIX])
                if l == 0:
                    dve.wait_ge(c2_in, 16)
                    dve.wait_ge(consts, 4)
                    note(V.tensor_copy(sel4[:, :, :], sel4_f))
                for t in range(NT):
                    await_drained(l, "mk", t)
                    await_drained(l, "mq", t)
                zh = zqk.rearrange("p t (h d) -> p t h d", d=HD)
                x1, x2 = zh[:, :, :, 0:8], zh[:, :, :, 8:16]
                cos, sin = (rope[:, i, :, :].unsqueeze(2).to_broadcast([P, NT, 16, 8]) for i in range(2))
                note(tt(rt[:, 0], x1, cos, ALU.mult))
                note(tt(rt[:, 1], x2, sin, ALU.mult))
                note(tt(rt[:, 2], x2, cos, ALU.mult))
                link(tt(rt[:, 3], x1, sin, ALU.mult))
                note(tt(x1, rt[:, 0], rt[:, 1], ALU.subtract))
                tt(x2, rt[:, 2], rt[:, 3], ALU.add).then_inc(rope_done, 1)
                b = await_full(l, "small")
                small = ((iT, 4), (fT, 4), (aT, 16))
                await_drained(l, "rb")
                for (p0, n), (dst, _) in zip(SMALL, small):
                    note(tt(dst[0:n, :], ps[p0:p0 + n, b, 0:T], rb[p0:p0 + n, :], ALU.mult))
                settle()
                for i, (dst, n) in enumerate(small):
                    ins = ts(dst[0:n, :], dst[0:n, :], cols[0:n, l, C_SB + i:C_SB + i + 1], None, ALU.add)
                    if i < 2:
                        note(ins)
                ins.then_inc(drained[b], 1)
                ahead(l, "mv")
                biased(l, "mv", lambda t: vm[:, t, :])
                for i in (2, 3):
                    b = await_full(l, "qkT", i)
                    V.tensor_copy(qkT[:, 2 * i:2 * i + 2, :], ps[:, b, :].rearrange("p (m n) -> p m n", m=2))\
                        .then_inc(drained[b], 1)
                ahead(l, "gqk")
                for i in range(2):
                    b = await_full(l, "gqk", i)
                    tt(gqk[:, 2 * i:2 * i + 2, :], ps[:, b, :].rearrange("p (m n) -> p m n", m=2),
                       rb.unsqueeze(1).to_broadcast([P, 2, T]), ALU.mult).then_inc(drained[b], 1)
                for m in range(4):
                    await_drained(l, "gqk", m // 2)
                    note(ts(gqk[:, m, :], gqk[:, m, :], cols[:, l, C_BG + m:C_BG + m + 1],
                            GD ** -0.5 if m < 2 else 1.0, ALU.add, ALU.mult))
                ahead(l, "gv")
                biased(l, "gv", lambda t: vg[:, t, :])
                soft_scores(l, 0)
                ahead(l, "gr")
                biased(l, "gr", lambda t: gr[:, t, :])
                soft_scores(l, 1)
                row_sums(l, 0)
                ahead(l, "lq")
                conv_rows(l, "lq")
                row_sums(l, 1)
                b = await_full(l, "ga")
                for m in range(2):
                    ins = ts(gz[:, m * T:(m + 1) * T], ps[:, b, m * T:(m + 1) * T],
                             cols[:, l, C_GB + m:C_GB + m + 1], None, ALU.add)
                ins.then_inc(drained[b], 1)
                await_drained(l, "ga")
                ahead(l, "lk")
                conv_rows(l, "lk")
                probs_out(l, 0)
                conv_taps(l, 0)
                ahead(l, "lv", 0)
                moba_rows(l, 0)
                ahead(l, "lv")
                probs_out(l, 1)
                biased(l, "lv", lambda t: vl[:, t, :])
                ahead(l, "lo", 0)
                dve.wait_ge(lsg2, l + 1)
                note(stt(cumf[0:4, :], fT[0:4, :], 0.0, cumf[0:4, :], ALU.min, ALU.subtract))
                link(stt(gA, gz, 0.0, gB, ALU.min, ALU.subtract))
                link(V.tensor_tensor_scan(gC, chunk_start[:, :], gA, 0.0, ALU.mult, ALU.add))
                gc = gC.rearrange("p (c n) -> p c n", n=CH)
                ce = gE.rearrange("p (c n) -> p c n", n=CH)
                tt(ce, gc[:, :, CH - 1:CH].to_broadcast([P, 2 * T // CH, CH]), gc, ALU.subtract).then_inc(gla_cum, 1)
                link(V.tensor_tensor_scan(fls[0:4, :], ones[0:4, 0:1].to_broadcast([4, T]), cumf[0:4, :], 0.0, ALU.mult, ALU.add))
                link(tt(gl[0:4, :], iT[0:4, :], fls[0:4, :], ALU.subtract))
                link(V.tensor_tensor_scan(rmax[0:4, :], gl[0:4, :], gl[0:4, :], 0.0, ALU.max, ALU.max))
                link(V.tensor_copy(rmax_hi[:, :], rmax[0:4, :]))
                note(tt(rmax_lo[:, :], rmax[0:4, :], rmax_hi[:, :], ALU.subtract))
                tt(fls[0:4, :], fls[0:4, :], rmax[0:4, :], ALU.add).then_inc(rows_ready, 1)
                conv_taps(l, 1)
                ahead(l, "lo")
                biased(l, "lo", lambda t: lo[:, t, :])
                moba_rows(l, 1)
                dve.wait_ge(gla_exp, l + 1)
                qd = gqk[:, 0:2, :]
                kk = gqk[:, 2:4, :]
                a3, b3, e3 = (v.rearrange("p (m n) -> p m n", m=2) for v in (gA, gB, gE))
                note(tt(b3, kk, b3, ALU.mult))
                note(tt(e3, kk, e3, ALU.mult))
                link(tt(qd, qd, a3, ALU.mult))
                for m in range(2):
                    e1, e2 = a3[:, m, 2 * CH - 1:2 * CH], a3[:, m, 3 * CH - 1:3 * CH]
                    note(ts(gx[:, m, 0:CH], qd[:, m, 2 * CH:3 * CH], e1, None, ALU.mult))
                    note(ts(gx[:, m, 2 * CH:3 * CH], qd[:, m, 3 * CH:4 * CH], e2, None, ALU.mult))
                settle()
                for m in range(2):
                    ins = ts(gx[:, m, CH:2 * CH], gx[:, m, 2 * CH:3 * CH], a3[:, m, 2 * CH - 1:2 * CH], None, ALU.mult)
                    if m:
                        ins.then_inc(gla_ops, 1)
                    else:
                        note(ins)
                ahead(l, "g0", 0)
                b = await_full(l, "lc")
                V.tensor_copy(lcol, ps[:, b, 0:16]).then_inc(drained[b], 1)
                ahead(l, "g0")
                biased(l, "g0", lambda t: gates[:, 0, t, :])
                dve.wait_ge(pads, 2 * l + 2)
                for h in range(4):
                    b = await_full(l, "gs", h)
                    V.copy_predicated(g_att[:, h, :], gmask[:, :], ps[:, b, 0:384]).then_inc(drained[b], 1)
                ahead(l, "g0'", 0)
                for i in range(2):
                    lo_of(l, "yT0", i, yT_hi, yT_lo)
                ahead(l, "g0'")
                biased(l, "g0'", lambda t: gates[:, 1, t, :])
                dve.wait_ge(gstat, 3 * l + 2)
                link(V.reduce_sum(gss, tmp[:, 0:2 * W].rearrange("p (h n) -> p h n", h=8), AX))
                ts(gvar, gss, 1.0 / 128, EPS, ALU.mult, ALU.add).then_inc(gstatv, 1)
                ahead(l, "up0", 0)
                dve.wait_ge(gstat, 3 * l + 3)
                rsqrt(gy0, gvar, gn0, grs)
                for t in range(NT):
                    b = await_full(l, "go", t)
                    tt(ytok[:, t, :].rearrange("p (h n) -> p h n", h=4), ps[:, b, :].rearrange("p (h n) -> p h n", h=4),
                       grs[:, 4 * t:4 * t + 4].unsqueeze(2).to_broadcast([P, 4, P]), ALU.mult).then_inc(drained[b], 1)
                merge(l, 0, 0)
                ahead(l, "up0")
                await_drained(l, "lc")
                for i in range(2):
                    b = await_full(l, "mb", i)
                    for hh in range(2):
                        h = 2 * i + hh
                        ts(mE[:, h, 0:T], ps[:, b, hh * T:(hh + 1) * T], lcol[:, h:h + 1], 0.0, ALU.subtract, ALU.max)
                        ins = ts(mE[:, h, T:T + P], ps[:, b, hh * T + P:(hh + 1) * T], lcol[:, 4 + h:5 + h], 0.0,
                                 ALU.subtract, ALU.max)
                    ins.then_inc(drained[b], 1)
                dve.wait_ge(gate_ready, NG * l + GATES["gr"])
                for t in range(NT):
                    await_drained(l, "go", t)
                    tt(ytok[:, t, :], ytok[:, t, :], gr[:, t, :], ALU.mult).then_inc(y_ready, 1)
                merge(l, 0, 1)
                dve.wait_ge(mEr, l + 1)
                note(tt(mE, mE, mmask[:, :].unsqueeze(1).to_broadcast([P, 4, 384]), ALU.mult))
                ahead(l, "g1", 0)
                for i in range(2):
                    lo_of(l, "yT1", i, yT_hi, yT_lo, C_GN)
                ahead(l, "g1")
                for i in range(2):
                    await_drained(l, "up0", i)
                biased(l, "g1", lambda t: gates[:, 0, t, :])
                settle()
                for h in range(4):
                    b = await_full(l, "ms", h)
                    stt(mW[:, h, :], ps[:, b, 0:384], MD ** -0.5, mE[:, h, :], ALU.mult, ALU.mult)\
                        .then_inc(drained[b], 1)
                ahead(l, "g1'")
                for i in range(2, 4):
                    await_drained(l, "up0", i)
                biased(l, "g1'", lambda t: gates[:, 1, t, :])
                ahead(l, "up1")
                merge(l, 1, 0)
                merge(l, 1, 1)
                b = await_full(l, "mo", 2)
                link(stt(lden, ps[:, b, 0:8], -1.0, lcol[:, 8:16], ALU.mult, ALU.max))
                tt(lden, ps[:, b, 0:8], lden, ALU.max).then_inc(drained[b], 1)
                await_drained(l, "mo", 2)
                link(V.reciprocal(lrin, lden))
                for t in range(NT):
                    b = await_full(l, "mo", t)
                    tt(ytok[:, t, :].rearrange("p (h n) -> p h n", h=4), ps[:, b, :].rearrange("p (h n) -> p h n", h=4),
                       lrin[:, 4 * t:4 * t + 4].unsqueeze(2).to_broadcast([P, 4, P]), ALU.mult).then_inc(drained[b], 1)
                dve.wait_ge(gate_ready, NG * l + GATES["lo"])
                for t in range(NT):
                    await_drained(l, "mo", t)
                    tt(ytok[:, t, :], ytok[:, t, :], lo[:, t, :], ALU.mult).then_inc(y_ready, 1)
                ahead(l, "g2")
                biased(l, "g2", lambda t: gates[:, 0, t, :])
                for i in range(2):
                    lo_of(l, "yT2", i, yT_hi, yT_lo)
                ahead(l, "g2'", 0)
                ahead(l, "up2", 0)
                merge(l, 2, 0)
                ahead(l, "g2'", 1)
                biased(l, "g2'", lambda t: gates[:, 1, t, :])
                for i in range(2):
                    lo_of(l, "mgT", i, hT_hi, hT_lo)
                ahead(l, "up2", 1)
                merge(l, 2, 1)
                ahead(l, "wo", 0)
                for i in range(2, 4):
                    lo_of(l, "mgT", i, hT_hi, hT_lo)
                if l == L - 1:
                    small_parts(L + 1, KT * E)
                ahead(l, "wo", 1)
                for h, name in enumerate(("wo", "wo'")):
                    for t in range(NT):
                        b = await_full(l, name, t)
                        r = xt[:, t, h * W:(h + 1) * W]
                        tt(r, r, ps[:, b, :], ALU.add).then_inc(drained[b], 1)
                    if h:
                        ahead(l, "wo'", 1)
                    for i in range(2 * h, 2 * h + 2):
                        lo_of(l, "fnorm", i, hT_hi, hT_lo, C_FG)
                norm(rstds[:, 2 * l + 1, :])
                if l == 0:
                    for n, (kind, i, c) in enumerate(FF):
                        if n != 1:
                            split_to(2 * NU + n + 2)
                        if kind == "gu" and c == 1:
                            for t in range(NT):
                                b = await_full(0, f"gu{i}", t)
                                nsilu[0] += 1
                                dve.wait_ge(silu_ready, nsilu[0])
                                stt(hid[:, t, :], ps[:, b, 256:512], rstds[:, 1, t:t + 1], silu_g[:, t, :],
                                    ALU.mult, ALU.mult).then_inc(drained[b], 1)
                        if kind == "dn" and i + 1 < NF or (kind, i, c) == ("gu", 1, 0):
                            i = i + 1 if kind == "dn" else 0
                            b = await_full(0, f"hT{i}")
                            nhi[0] += 1
                            dve.wait_ge(hi_part, nhi[0])
                            r = slice(2 * (i % 2), 2 * (i % 2) + 2)
                            tt(yT_lo[:, r, :], ps[:, b, :].rearrange("p (m n) -> p m n", m=2), yT_hi[:, r, :],
                               ALU.subtract).then_inc(drained[b], 1)
                    for t in range(NT):
                        b = await_full(0, "acc", t)
                        tt(xt[:, t, 0:W], xt[:, t, 0:W], ps[:, b, :], ALU.add).then_inc(drained[b], 1)

            def split_moe(pas, e, j):
                dve.wait_ge(hi_ready, e * FFC + (MOE_BASE + pas * E * FFC + j + 1))
                tt(w_lo[:, j % RS, :], slot_raw(j, True), w_hi[:, j % RS, :], ALU.subtract).then_inc(lo_ready, 1)

            dve.wait_ge(moe_consts, 2)
            dve.wait_ge(fg_in, 48)
            note(V.tensor_copy(iota, iota_i))
            r = rstds[:, 2 * L - 1, :]

            def rows(t):
                note(stt(xn[:, t, :], xt[:, t, :], r[:, t:t + 1], ffn_g, ALU.mult, ALU.mult))

            b = await_full(1, "lgT")
            for t in range(NT):
                ins = stt(lg[:, t, :], ps[:, b, t * E:(t + 1) * E], r[:, t:t + 1], rbias, ALU.mult, ALU.add)
            ins.then_inc(drained[b], 1)
            await_drained(1, "lgT")
            for t in range(NT):
                note(V.max(m8[:, t, :], lg[:, t, :]))
            settle()
            tt(g12[:, :, 0:1], m8[:, :, 1:2], m8[:, :, 0:1], ALU.subtract).then_inc(router_d2, 1)
            for t in range(NT):
                note(V.max_index(idx[:, t, :], m8[:, t, :], lg[:, t, :]))
            settle()
            link(V.tensor_copy(idf, idx))
            for t in range(NT):
                for a in range(2):
                    note(ts(oh[:, a, t, :], iota[:, 0:E], idf[:, t, a:a + 1], None, ALU.is_equal))
            settle()
            tt(ind, oh[:, 0, :, :], oh[:, 1, :, :], ALU.add).then_inc(ind_ready, 1)
            for t in range(NT):
                rows(t)
            b = await_full(1, "rank")
            dve.wait_ge(ind_ready, 1)
            note(stt(pos[:, :, 0:E], ps[:, b, 0:NT * E].rearrange("p (t n) -> p t n", t=NT), 1.0, ind, ALU.add, ALU.mult))
            V.reduce_max(g12[:, 1, 3:4], ps[:, b, 2 * E:3 * E], AX).then_inc(drained[b], 1)
            await_drained(1, "rank")
            settle()
            note(ts(pos[:, :, E:2 * E], pos[:, :, 0:E], -1.0 - P, None, ALU.add))
            link(ts(pos[:, :, 0:E], pos[:, :, 0:E], -1.0, None, ALU.add))
            V.tensor_copy(cnt_i[:, :], g12[:, 1, 3:4]).then_inc(pos_ready, 1)

            def gates_of_picks():
                dve.wait_ge(pos_ready, 1)
                dve.wait_ge(router_e, 1)
                link(ts(g12[:, :, 3:4], g12[:, :, 0:1], 1.0, None, ALU.add))
                link(V.reciprocal(g12[:, :, 1:2], g12[:, :, 3:4]))
                link(tt(g12[:, :, 2:3], g12[:, :, 0:1], g12[:, :, 1:2], ALU.mult))
                for t in range(NT):
                    for a in range(2):
                        note(ts(oh[:, a, t, :], oh[:, a, t, :], g12[:, t, 1 + a:2 + a], None, ALU.mult))
                settle()
                for s in range(2):
                    note(tt(gmat[:, :, s * E:(s + 1) * E], oh[:, 0, :, :], oh[:, 1, :, :], ALU.add))
                settle()

            def select(col):
                for t in range(NT):
                    ins = ts(sel[:, t, :], iota, pos[:, t, col], None, ALU.is_equal)
                ins.then_inc(sel_ready, 1)

            def gather_lo(banks, waits, nh):
                for i in range(2):
                    dve.wait_ge(full[banks[i]], waits[i])
                    dve.wait_ge(hi_part, nh + i + 1)
                    r = slice(4 * i, 4 * i + 4)
                    tt(hT_lo[:, r, 0:P], ps[:, banks[i], :].rearrange("p (m n) -> p m n", m=4), hT_hi[:, r, 0:P],
                       ALU.subtract).then_inc(drained[banks[i]], 1)

            HI0 = nhi[0]
            HIX = NF + 4

            def moe_pass(pas):
                base = PASS_FILL[pas]
                hb = HI0 + pas * (2 + E * HIX)
                select(slice(pas * E, pas * E + 1))
                for j in range(2):
                    split_moe(pas, 0, j)
                gather_lo((6, 7), (base[6] + 1, base[7] + 1), hb)
                if pas == 0:
                    gates_of_picks()
                V.tensor_copy(gcur.unsqueeze(2), gmat[:, :, pas * E:pas * E + 1])
                for v in (selT, ysb_hi, ysb_lo):
                    ins = V.tensor_copy(v, zeros.unsqueeze(1).to_broadcast([P, v.shape[1], P]))
                ins.then_inc(zeroed, 1)

                def add_rows(t, fill):
                    for h in range(2):
                        b, k = fill(h)
                        dve.wait_ge(full[b], k + 1)
                        dve.wait_ge(drained[b], k)
                        r = xt[:, t, h * W:(h + 1) * W]
                        tt(r, r, ps[:, b, :], ALU.add).then_inc(drained[b], 1)

                def expert(e, last):
                    nh = 0

                    def moe_full(tag, i=0):
                        b, k = moe_fill(pas, e, tag, i)
                        dve.wait_ge(full[b], k + 1)
                        return b

                    for n, (kind, i, c) in enumerate(FF):
                        if n not in (1, 3) and (n + 2 < FFC or not last):
                            split_moe(pas, e, n + 2)
                        if n == FFC - 1:
                            fb = [moe_fill(pas, e, "gather", q) for q in range(2)]
                            gather_lo([f[0] for f in fb], [f[1] + 1 for f in fb], e * HIX + (hb + 2 + nh))
                            nh += 2
                            for h in range(2):
                                b = moe_full("acc", h)
                                dve.wait_ge(hi_part, e * HIX + (hb + 2 + nh + 1))
                                nh += 1
                                stt(ysb_lo[:, 4 * h:4 * h + 4, :], ps[:, b, :].rearrange("p (m n) -> p m n", m=4),
                                    gslot, ysb_hi[:, 4 * h:4 * h + 4, :], ALU.mult, ALU.subtract)\
                                    .then_inc(drained[b], 1)
                        if kind == "gu" and c == 1:
                            b = moe_full(f"gu{i}")
                            dve.wait_ge(silu_ready, e * NF + (NT * NF + pas * E * NF + i + 1))
                            tt(hid[:, i % 2, :], silu_g[:, i % 2, :], ps[:, b, 256:512], ALU.mult)\
                                .then_inc(drained[b], 1)
                            if n in (1, 3):
                                split_moe(pas, e, n + 2)
                        if (kind, i, c) == ("gu", 2, 0):
                            add_rows(1, lambda h: moe_fill(pas, e, "sc1", h))
                        if kind == "dn" and i + 1 < NF or (kind, i, c) == ("gu", 1, 0):
                            ih = i + 1 if kind == "dn" else 0
                            b = moe_full(f"hT{ih}")
                            dve.wait_ge(hi_part, e * HIX + (hb + 2 + nh + 1))
                            nh += 1
                            r = slice(2 * (ih % 2), 2 * (ih % 2) + 2)
                            tt(yT_lo[:, r, 0:P], ps[:, b, 0:2 * P].rearrange("p (m n) -> p m n", m=2),
                               yT_hi[:, r, 0:P], ALU.subtract).then_inc(drained[b], 1)
                            if kind == "gu":
                                add_rows(0, lambda h: moe_fill(pas, e, "sc0", h))
                        if kind == "dn" and i == 4:
                            b = moe_full("selT")
                            V.tensor_copy(gslot, ps[:, b, T:T + 1])
                            V.tensor_copy(selT, ps[:, b, 0:T].rearrange("p (t n) -> p t n", t=NT))\
                                .then_inc(drained[b], 1)
                            V.tensor_copy(gcur.unsqueeze(2), gmat[:, :, bass.ds(e + (pas * E + 1), 1)])
                            select(bass.ds(e + (pas * E + 1), 1))
                    assert nh == HIX

                with dve.Fori(0, E - 1) as e:
                    expert(e, False)
                expert(E - 1, True)
                for t in range(NT):
                    add_rows(t, lambda h: (6 + h, base[6 + h] + PRO[6] + E * nexp[6 + h] + t))
                for q in (6, 7):
                    dve.wait_ge(drained[q], base[q] + PRO[q] + E * nexp[q] + EPI[q])

            moe_pass(0)
            many = dve.value_load(cnt_i[0:1, 0:1], min_val=0, max_val=T)
            with dve.If(many > P):
                moe_pass(1)
            for h in range(2):
                c = slice(h * W, (h + 1) * W)
                for t in range(NT):
                    tt(xn[:, t, c], xt[:, t, c], fin_g[:, c], ALU.mult).then_inc(final_rows, 1)
            norm(rfin, rfin_ready)
            for h in range(2):
                c = slice(h * W, (h + 1) * W)
                ts(xn[:, 0, c], xn[:, 0, c], rfin[:, 0:1], None, ALU.mult).then_inc(scaled[0], 1)


def kernel(**inputs):
    import concourse.bacc as bacc
    from concourse import mybir
    from concourse.bass_utils import run_bass_kernel_spmd

    L, D, _ = inputs["w_in"].shape
    T, P, KT = inputs["x"].shape[1], 128, D // 128
    a = {k: np.ascontiguousarray(v) for k, v in inputs.items()}

    def column(v, tiles):
        return v.reshape(L, tiles, P).transpose(0, 2, 1)

    b = a["b_in"]
    conv_w = a["mlstm_conv_w"].transpose(0, 2, 1).reshape(L, 8, P, 4).transpose(0, 2, 1, 3).reshape(L, P, 32)
    w_small = np.zeros((L, P, KT, 80), np.float32)
    b_small = np.zeros((L, P, 3), np.float32)
    for i, (at, src, n) in enumerate(((0, 4624, 4), (32, 4628, 4), (64, 2560, 16))):
        w_small[:, :, :, at:at + n] = a["w_in"][:, :, src:src + n].reshape(L, KT, P, n).transpose(0, 2, 1, 3)
        b_small[:, 0:n, i] = b[:, src:src + n]
    w_small = w_small.reshape(L, P, KT * 80)
    cols = np.concatenate([column(a["attn_norm_g"], KT), column(a["ffn_norm_g"], KT), conv_w,
                           column(a["mlstm_conv_b"], 8), column(b[:, 1536:2048], 4), column(b[:, 3088:4112], 8),
                           column(a["gla_gate_b"], 2), column(a["gla_norm_g"], 4), b_small], axis=2)
    router = a["router_w"][0].reshape(KT, P, -1).transpose(1, 0, 2).reshape(P, -1)
    inv = np.power(np.float32(500000.0), -np.arange(8, dtype=np.float32) * np.float32(2.0) / np.float32(16))
    ang = np.arange(T, dtype=np.float32)[:, None] * inv[None, :].astype(np.float32)
    rope = np.stack([np.cos(ang), np.sin(ang)]).astype(np.float32)
    rope = rope.reshape(2, T // P, P, 8).transpose(2, 0, 1, 3)

    nc = bacc.Bacc("TRN2", target_bir_lowering=False, num_devices=1)
    arrays = {}

    def dram(name, v):
        v = np.ascontiguousarray(v)
        arrays[name + "_dram"] = v
        return nc.dram_tensor(name + "_dram", v.shape, mybir.dt.from_np(v.dtype), kind="ExternalInput").ap()

    args = [dram("x", a["x"][0]), dram("w_in", a["w_in"]), dram("b_in", b), dram("cols", cols),
            dram("w_small", w_small), dram("gate_w", a["gla_gate_w"]),
            [dram(n, a[n]) for n in ("w_up_moba", "w_up_gla", "w_up_mlstm")], dram("w_o", a["w_o"]),
            dram("ffn_gate", a["ffn_w_gate"][0]), dram("ffn_up", a["ffn_w_up"][0]), dram("ffn_down", a["ffn_w_down"][0]),
            dram("router", router), dram("router_b", a["router_b"][0]), dram("moe_gate", a["moe_w_gate"][0]),
            dram("moe_up", a["moe_w_up"][0]), dram("moe_down", a["moe_w_down"][0]),
            dram("ffn_norm_g", a["ffn_norm_g"]), dram("final_g", a["final_norm_g"]), dram("rope", rope)]
    out = nc.dram_tensor("out_dram", (T, D), mybir.dt.float32, kind="ExternalOutput").ap()
    program(nc, *args, out)
    r = run_bass_kernel_spmd(nc, [arrays], core_ids=[0])
    return r.results[0]["out_dram"].reshape(1, T, D)
```
